# Optimizing a Trainium2 kernel written in Bass

```python
import jax, jax.numpy as jnp
from jax import lax
import numpy as np
import math

D_MODEL = 1024
BATCH = 1
SEQ = 512
DEPTH = 2

CHUNK = 64
N_META = 16
CONV_WIDTH = 3
D_CONV = D_MODEL
N_RET_HEADS = 4
RET_QK_DIM = 256
RET_V_DIM = 512
D_RET_QK = N_RET_HEADS * RET_QK_DIM
D_RET_V = N_RET_HEADS * RET_V_DIM
ROPE_BASE = 10000.0
RMS_EPS = 1e-6
GN_EPS = 1e-5
D_IN = 4 * D_CONV + 2 * D_RET_QK + 2 * D_RET_V + 2 * D_MODEL


def _rmsnorm(x, g):
    xf = x.astype(jnp.float32)
    y = xf * lax.rsqrt(jnp.mean(xf * xf, axis=-1, keepdims=True) + RMS_EPS)
    return (y * g.astype(jnp.float32)).astype(x.dtype)

def _rope(x, pos):
    half = x.shape[-1] // 2
    inv = ROPE_BASE ** (-jnp.arange(half, dtype=jnp.float32) / half)
    ang = pos[:, None] * inv[None, :]
    cos = jnp.cos(ang)[None, :, None, :]
    sin = jnp.sin(ang)[None, :, None, :]
    x1, x2 = x[..., :half], x[..., half:]
    return jnp.concatenate([x1 * cos - x2 * sin, x1 * sin + x2 * cos], axis=-1)

def _short_conv_branch(h, gb, gc, z, conv_w, conv_b, w_out):
    u = gc * h
    up = jnp.pad(u, ((0, 0), (CONV_WIDTH - 1, 0), (0, 0)))
    T = u.shape[1]
    y = conv_b + sum(conv_w[j] * up[:, j:j + T] for j in range(CONV_WIDTH))
    y = gb * y * jax.nn.silu(z)
    return y @ w_out

def _retention_branch(q, k, v, z, gn_g, w_out):
    Bsz, T, _ = q.shape
    H, dk, dv = N_RET_HEADS, RET_QK_DIM, RET_V_DIM
    pos = jnp.arange(T, dtype=jnp.float32)
    qf = _rope(q.astype(jnp.float32).reshape(Bsz, T, H, dk), pos)
    kf = _rope(k.astype(jnp.float32).reshape(Bsz, T, H, dk), pos) * (dk ** -0.5)
    vf = v.astype(jnp.float32).reshape(Bsz, T, H, dv)
    n_pad = (-N_META) % CHUNK
    padw = ((0, 0), (n_pad, 0), (0, 0), (0, 0))
    qf, kf, vf = (jnp.pad(a, padw) for a in (qf, kf, vf))
    L = T + n_pad
    n_chunks = L // CHUNK

    def to_chunks(a):
        return a.reshape(Bsz, n_chunks, CHUNK, H, a.shape[-1]).transpose(1, 0, 3, 2, 4)

    qc, kc, vc = to_chunks(qf), to_chunks(kf), to_chunks(vf)
    log_g = jnp.log(1.0 - 2.0 ** (-5.0 - jnp.arange(H, dtype=jnp.float32)))
    idx = jnp.arange(CHUNK, dtype=jnp.float32)
    intra_dec = jnp.exp(log_g[:, None, None] * jnp.abs(idx[:, None] - idx[None, :]))
    q_dec = jnp.exp(log_g[:, None] * (idx + 1.0))[None, :, :, None]
    k_dec = jnp.exp(log_g[:, None] * (CHUNK - 1.0 - idx))[None, :, :, None]
    chunk_dec = jnp.exp(log_g * CHUNK)[None, :, None, None]

    def step(state, inp):
        qi, ki, vi = inp
        s = jnp.einsum('bhnd,bhmd->bhnm', qi, ki) * intra_dec
        intra = jnp.einsum('bhnm,bhmv->bhnv', s, vi)
        cross = jnp.einsum('bhnd,bhdv->bhnv', qi * q_dec, state)
        new_state = state * chunk_dec + jnp.einsum('bhmd,bhmv->bhdv', ki * k_dec, vi)
        return new_state, intra + cross

    state0 = jnp.zeros((Bsz, H, dk, dv), jnp.float32)
    _, out = lax.scan(step, state0, (qc, kc, vc))
    out = out.transpose(1, 0, 3, 2, 4).reshape(Bsz, L, H, dv)[:, n_pad:]
    mu = jnp.mean(out, axis=-1, keepdims=True)
    var = jnp.mean(jnp.square(out - mu), axis=-1, keepdims=True)
    out = (out - mu) * lax.rsqrt(var + GN_EPS) * gn_g.astype(jnp.float32).reshape(H, dv)
    out = out.reshape(Bsz, T, D_RET_V).astype(z.dtype) * jax.nn.silu(z)
    return out @ w_out

def first_inputs(seed: int = 0) -> dict:
    key = jax.random.key(seed)
    ks = jax.random.split(key, 16)
    nrm = jax.random.normal
    f32 = jnp.float32
    return {
        "x": nrm(ks[0], (BATCH, SEQ, D_MODEL), f32),
        "meta": nrm(ks[1], (N_META, D_MODEL), f32),
        "pre_norm_g": 1.0 + 0.05 * nrm(ks[2], (DEPTH, D_MODEL), f32),
        "w_in": nrm(ks[3], (DEPTH, D_MODEL, D_IN), f32) * D_MODEL ** -0.5,
        "b_in": 0.02 * nrm(ks[4], (DEPTH, D_IN), f32),
        "conv_w": nrm(ks[5], (DEPTH, CONV_WIDTH, D_CONV), f32) * CONV_WIDTH ** -0.5,
        "conv_b": 0.02 * nrm(ks[6], (DEPTH, D_CONV), f32),
        "w_conv_out": nrm(ks[7], (DEPTH, D_CONV, D_MODEL), f32) * D_CONV ** -0.5,
        "ret_gn_g": 1.0 + 0.05 * nrm(ks[8], (DEPTH, D_RET_V), f32),
        "w_ret_out": nrm(ks[9], (DEPTH, D_RET_V, D_MODEL), f32) * D_RET_V ** -0.5,
        "w_o": nrm(ks[10], (DEPTH, D_MODEL, D_MODEL), f32) * D_MODEL ** -0.5,
        "post_norm_g": 1.0 + 0.05 * nrm(ks[11], (DEPTH, D_MODEL), f32),
    }

def first_block(x, meta, pre_norm_g, w_in, b_in, conv_w, conv_b, w_conv_out,
              ret_gn_g, w_ret_out, w_o, post_norm_g):
    Bsz = x.shape[0]
    meta_b = jnp.broadcast_to(meta[None].astype(x.dtype), (Bsz, N_META, D_MODEL))
    h = jnp.concatenate([meta_b, x], axis=1)
    sizes = (D_CONV,) * 4 + (D_RET_QK,) * 2 + (D_RET_V,) * 2 + (D_MODEL,) * 2
    split_at = [int(s) for s in np.cumsum(sizes)[:-1]]
    for l in range(DEPTH):
        xn = _rmsnorm(h, pre_norm_g[l])
        proj = xn @ w_in[l] + b_in[l]
        c_h, c_b, c_c, c_z, r_q, r_k, r_v, r_z, g_a, g_b = jnp.split(proj, split_at, axis=-1)
        y_a = _short_conv_branch(c_h, c_b, c_c, c_z, conv_w[l], conv_b[l], w_conv_out[l])
        y_b = _retention_branch(r_q, r_k, r_v, r_z, ret_gn_g[l], w_ret_out[l])
        y = jax.nn.sigmoid(g_a) * y_a + jax.nn.sigmoid(g_b) * y_b
        y = y @ w_o[l]
        h = h + _rmsnorm(y, post_norm_g[l])
    return h[:, N_META:]


DEPTH_2 = 1

HG_HEADS = 4
HG_HEAD_K = 128
HG_HEAD_V = 128
HG_KEY = HG_HEADS * HG_HEAD_K
HG_VAL = HG_HEADS * HG_HEAD_V
GLA_HEADS = 4
GLA_HEAD_K = 64
GLA_HEAD_V = 128
GLA_KEY = GLA_HEADS * GLA_HEAD_K
GLA_VAL = GLA_HEADS * GLA_HEAD_V
GLA_GATE_RANK = 16
GLA_GATE_NORMALIZER = 16.0
MIX_WIDTH = HG_VAL + GLA_VAL
IN_SPLITS = (HG_KEY, HG_KEY, HG_VAL, HG_VAL, GLA_KEY, GLA_KEY, GLA_VAL, GLA_GATE_RANK, GLA_VAL)
IN_WIDTH = sum(IN_SPLITS)
PEER_HEADS = 8
PEER_N_KEYS = 128
PEER_N_EXPERTS = PEER_N_KEYS * PEER_N_KEYS
PEER_QUERY_DIM = 256
PEER_HALF = PEER_QUERY_DIM // 2
PEER_TOPK = 16
PEER_BLOCK = 128
EPS = 1e-6


def rms_norm(x, g):
    xf = x.astype(jnp.float32)
    y = xf * lax.rsqrt(jnp.mean(xf * xf, axis=-1, keepdims=True) + EPS)
    return (y * g.astype(jnp.float32)).astype(x.dtype)

def split_heads(a, n_heads):
    b, t, w = a.shape
    return a.reshape(b, t, n_heads, w // n_heads).transpose(0, 2, 1, 3)

def merge_heads(a):
    b, n, t, d = a.shape
    return a.transpose(0, 2, 1, 3).reshape(b, t, n * d)

def chunk_gated_linear_attention(q, k, v, log_g):
    b, h, t, dk = q.shape
    dv = v.shape[-1]
    n_chunks = t // CHUNK

    def to_chunks(a):
        return a.astype(jnp.float32).reshape(b, h, n_chunks, CHUNK, a.shape[-1]).transpose(2, 0, 1, 3, 4)

    qc, kc, vc, gc = to_chunks(q), to_chunks(k), to_chunks(v), to_chunks(log_g)
    causal = jnp.tril(jnp.ones((CHUNK, CHUNK), dtype=bool))[:, :, None]

    def step(state, inp):
        qb, kb, vb, gb = inp
        cum = jnp.cumsum(gb, axis=2)
        rel = cum[:, :, :, None, :] - cum[:, :, None, :, :]
        decay = jnp.exp(jnp.where(causal, rel, -jnp.inf))
        scores = jnp.einsum('bhid,bhjd,bhijd->bhij', qb, kb, decay)
        out = (jnp.einsum('bhij,bhjv->bhiv', scores, vb)
               + jnp.einsum('bhid,bhdv->bhiv', qb * jnp.exp(cum), state))
        last = cum[:, :, -1:, :]
        state = (jnp.exp(last[:, :, 0, :])[..., None] * state
                 + jnp.einsum('bhjd,bhjv->bhdv', kb * jnp.exp(last - cum), vb))
        return state, out

    s0 = jnp.zeros((b, h, dk, dv), jnp.float32)
    _, o = lax.scan(step, s0, (qc, kc, vc, gc))
    return o.transpose(1, 2, 0, 3, 4).reshape(b, h, t, dv)

def hgrn2_mixer(q, f, i, gate, lower_bound, norm_g):
    q = jax.nn.silu(q)
    forget = lower_bound + (1.0 - lower_bound) * jax.nn.sigmoid(f.astype(jnp.float32))
    key = 1.0 - forget
    log_f = jnp.log(forget)
    o = chunk_gated_linear_attention(split_heads(q, HG_HEADS), split_heads(key, HG_HEADS),
                                     split_heads(i, HG_HEADS), split_heads(log_f, HG_HEADS))
    o = merge_heads(rms_norm(o, norm_g))
    return (o * jax.nn.silu(gate.astype(jnp.float32))).astype(gate.dtype)

def gla_mixer(q, k, v, gate_low, gate, w_gate_up, b_gate, norm_g):
    log_g = jax.nn.log_sigmoid((gate_low @ w_gate_up + b_gate).astype(jnp.float32)) / GLA_GATE_NORMALIZER
    q = q * (GLA_HEAD_K ** -0.5)
    o = chunk_gated_linear_attention(split_heads(q, GLA_HEADS), split_heads(k, GLA_HEADS),
                                     split_heads(v, GLA_HEADS), split_heads(log_g, GLA_HEADS))
    o = merge_heads(rms_norm(o, norm_g))
    return (o * jax.nn.silu(gate.astype(jnp.float32))).astype(gate.dtype)

def peer_ffn(xn, w_q, sub_keys, u, v):
    b, t, d = xn.shape
    blocks = xn.reshape(-1, PEER_BLOCK, d)

    def block(xb):
        q = (xb @ w_q).reshape(PEER_BLOCK, PEER_HEADS, 2, PEER_HALF)
        s = jnp.einsum('thpd,hpnd->thpn', q, sub_keys).astype(jnp.float32)
        s_top, i_top = lax.top_k(s, PEER_TOPK)
        cand = s_top[:, :, 0, :, None] + s_top[:, :, 1, None, :]
        cand_idx = i_top[:, :, 0, :, None] * PEER_N_KEYS + i_top[:, :, 1, None, :]
        cand = cand.reshape(PEER_BLOCK, PEER_HEADS, PEER_TOPK * PEER_TOPK)
        cand_idx = cand_idx.reshape(PEER_BLOCK, PEER_HEADS, PEER_TOPK * PEER_TOPK)
        best, pos = lax.top_k(cand, PEER_TOPK)
        expert = jnp.take_along_axis(cand_idx, pos, axis=-1)
        g = jax.nn.softmax(best, axis=-1)
        act = jax.nn.gelu(jnp.einsum('td,thkd->thk', xb, u[expert]), approximate=False)
        return jnp.einsum('thk,thkd->td', (g * act).astype(xb.dtype), v[expert])

    return lax.map(block, blocks).reshape(b, t, d)

def second_inputs(seed: int = 0) -> dict:
    key = jax.random.key(seed)
    ks = jax.random.split(key, 16)
    nrm = jax.random.normal
    L = DEPTH_2
    return {
        "x": nrm(ks[0], (BATCH, SEQ, D_MODEL), jnp.float32),
        "norm1_g": 1.0 + 0.02 * nrm(ks[1], (L, D_MODEL), jnp.float32),
        "w_in": nrm(ks[2], (L, D_MODEL, IN_WIDTH), jnp.float32) * D_MODEL ** -0.5,
        "hg_lower_logits": 0.1 * nrm(ks[3], (L + 1, HG_KEY), jnp.float32),
        "hg_norm_g": 1.0 + 0.02 * nrm(ks[4], (L, HG_HEAD_V), jnp.float32),
        "gla_w_gate_up": nrm(ks[5], (L, GLA_GATE_RANK, GLA_KEY), jnp.float32) * GLA_GATE_RANK ** -0.5,
        "gla_b_gate": 0.1 * nrm(ks[6], (L, GLA_KEY), jnp.float32),
        "gla_norm_g": 1.0 + 0.02 * nrm(ks[7], (L, GLA_HEAD_V), jnp.float32),
        "w_out": nrm(ks[8], (L, MIX_WIDTH, D_MODEL), jnp.float32) * MIX_WIDTH ** -0.5,
        "norm2_g": 1.0 + 0.02 * nrm(ks[9], (L, D_MODEL), jnp.float32),
        "peer_w_q": nrm(ks[10], (L, D_MODEL, PEER_HEADS * PEER_QUERY_DIM), jnp.float32) * D_MODEL ** -0.5,
        "peer_sub_keys": nrm(ks[11], (L, PEER_HEADS, 2, PEER_N_KEYS, PEER_HALF), jnp.float32) * PEER_HALF ** -0.5,
        "peer_u": nrm(ks[12], (L, PEER_N_EXPERTS, D_MODEL), jnp.float32) * D_MODEL ** -0.5,
        "peer_v": nrm(ks[13], (L, PEER_N_EXPERTS, D_MODEL), jnp.float32) * 0.3,
        "norm_f_g": 1.0 + 0.02 * nrm(ks[14], (D_MODEL,), jnp.float32),
    }

def second_block(x, norm1_g, w_in, hg_lower_logits, hg_norm_g, gla_w_gate_up, gla_b_gate, gla_norm_g,
              w_out, norm2_g, peer_w_q, peer_sub_keys, peer_u, peer_v, norm_f_g):
    lower_bounds = jnp.cumsum(jax.nn.softmax(hg_lower_logits.astype(jnp.float32), axis=0), axis=0)
    offsets = [int(o) for o in np.cumsum(IN_SPLITS)[:-1]]
    h = x
    for layer in range(DEPTH_2):
        xn = rms_norm(h, norm1_g[layer])
        proj = xn @ w_in[layer]
        hq, hf, hi, hgate, gq, gk, gv, glow, ggate = jnp.split(proj, offsets, axis=-1)
        o_hgrn = hgrn2_mixer(hq, hf, hi, hgate, lower_bounds[layer], hg_norm_g[layer])
        o_gla = gla_mixer(gq, gk, gv, glow, ggate, gla_w_gate_up[layer], gla_b_gate[layer], gla_norm_g[layer])
        mixed = jnp.concatenate([o_hgrn, o_gla], axis=-1)
        h = h + (mixed @ w_out[layer]).astype(h.dtype)
        hn = rms_norm(h, norm2_g[layer])
        h = h + peer_ffn(hn, peer_w_q[layer], peer_sub_keys[layer], peer_u[layer], peer_v[layer]).astype(h.dtype)
    return rms_norm(h, norm_f_g)


def setup_inputs(seed=0):
    out = dict(first_inputs(seed))
    for name, value in second_inputs(seed + 1).items():
        if name != "x":
            out[name + "_2"] = value
    return out


def reference(
    x, meta, pre_norm_g, w_in, b_in, conv_w, conv_b, w_conv_out, ret_gn_g, w_ret_out, w_o,
    post_norm_g, norm1_g_2, w_in_2, hg_lower_logits_2, hg_norm_g_2, gla_w_gate_up_2,
    gla_b_gate_2, gla_norm_g_2, w_out_2, norm2_g_2, peer_w_q_2, peer_sub_keys_2, peer_u_2,
    peer_v_2, norm_f_g_2,
):
    x = first_block(
        x, meta, pre_norm_g, w_in, b_in, conv_w, conv_b, w_conv_out, ret_gn_g, w_ret_out, w_o,
        post_norm_g,
    )
    return second_block(
        x, norm1_g_2, w_in_2, hg_lower_logits_2, hg_norm_g_2, gla_w_gate_up_2, gla_b_gate_2,
        gla_norm_g_2, w_out_2, norm2_g_2, peer_w_q_2, peer_sub_keys_2, peer_u_2, peer_v_2,
        norm_f_g_2,
    )


_drawn_inputs = setup_inputs


def setup_inputs(seed=0):
    import zlib

    import numpy as np

    out = dict(_drawn_inputs(seed))
    spreads = {}
    factors = {'norm1_g_2': 3.716,
     'hg_lower_logits_2': 8.0,
     'hg_norm_g_2': 35.663,
     'gla_b_gate_2': 4.034,
     'gla_norm_g_2': 34.684,
     'norm2_g_2': 35.592,
     'norm_f_g_2': 8.119}
    for name, (base, spread) in spreads.items():
        noise = np.random.default_rng([zlib.crc32(name.encode()), seed]).standard_normal(out[name].shape)
        drawn = base * np.exp(spread * noise) if base else spread * noise
        out[name] = __import__('jax').numpy.asarray(drawn.astype(out[name].dtype))
    for name, factor in factors.items():
        out[name] = (out[name] * factor).astype(out[name].dtype)
    return out
```

```python
from contextlib import ExitStack

import concourse.bass as bass
from concourse import mybir

F32 = mybir.dt.float32
R32 = mybir.dt.float32r
U32 = mybir.dt.uint32
U8 = mybir.dt.uint8
ALU = mybir.AluOpType
ACT = mybir.ActivationFunctionType
AX = mybir.AxisListType

T = 528
NM = 16
KB = 2048
NRAW = 3
DEPTH = 2
EPS = 1e-6
GN_EPS = 1e-5
LOWEST = -3.0e38
BLOCKS_LAYER = 64
BLOCKS_SECOND = 26
NSLOT = 11
AHEAD = 6


class Queue:

    def __init__(self, engine, sem, serial=False):
        self.engine, self.sem, self.n, self.seen, self.serial = engine, sem, 0, {}, serial

    def wait(self, *marks):
        for m in marks:
            if m is None:
                continue
            if isinstance(m, list):
                self.wait(*m)
                continue
            sem, value = m
            if self.seen.get(id(sem), 0) < value:
                self.seen[id(sem)] = value
                self.engine.wait_ge(sem, value)

    def op(self, fn, *marks):
        self.wait(*marks)
        if self.serial and self.n:
            self.wait((self.sem, self.n))
        self.n += 1
        fn(self.engine).then_inc(self.sem, 1)
        return (self.sem, self.n)

    def quiet(self, fn, *marks):
        self.wait(*marks)
        fn(self.engine)

    def dma(self, slot, out, in_, *marks):
        self.wait(*marks)
        slot[1] += 16
        self.engine.dma_start(out, in_).then_inc(slot[0], 16)
        return (slot[0], slot[1])


class Ring:

    def __init__(self, n):
        self.n, self.at, self.freed = n, 0, [None] * n

    def take(self):
        i = self.at % self.n
        self.at += 1
        return i, self.freed[i]


def two_blocks(nc, d):
    ctx = ExitStack()
    with ctx:
        sems = []

        def sem(name):
            s = ctx.enter_context(nc.semaphore(name))
            sems.append(s)
            return s

        def slot(name):
            return [sem(name), 0]

        PE = Queue(nc.tensor, sem("q_pe"))
        V = Queue(nc.vector, sem("q_dve"), True)
        A = Queue(nc.scalar, sem("q_act"), True)
        G = Queue(nc.gpsimd, sem("q_pool"))
        SP = Queue(nc.sync, sem("q_sp"))

        base = nc.sbuf_base
        base += (-base) % 64
        top = [base]

        def at(name, shape, dt, off):
            return nc.alloc_sbuf_tensor_at(name, shape, dt, offset=off)

        def put(name, shape, dt=F32):
            size = 4 if dt != U8 else 1
            for s in shape[1:]:
                size *= s
            off = top[0]
            top[0] += size + (-size) % 32
            return at(name, shape, dt, off)

        def area(size):
            off = top[0]
            top[0] += size + (-size) % 32
            return off

        w_area = area(0)
        RAW = put("RAW", [128, NRAW, KB])
        WH = put("WH", [128, 2, KB], R32)
        WL = put("WL", [128, 2, KB], R32)
        x_area = area(0)
        XH = put("XH", [128, 8, T], R32)
        XL = put("XL", [128, 8, T], R32)
        I128 = put("I128", [128, 128])
        BIN = put("BIN", [128, 96])
        CW = put("CW", [128, 24])
        CB = put("CB", [128, 8])
        GNG = put("GNG", [128, 16])
        LGT = put("LGT", [128, 8])
        LBS = put("LBS", [128, 6, 4])
        VG = put("VG", [128, 4])
        SS = put("SS", [128, 8])
        RS = put("RS", [128, 8])
        GBC = put("GBC", [128, 1024])
        HM = put("HM", [16, 1024])
        H = put("H", [128, 4, 1024])
        h_area = top[0] - 20480
        r_area = top[0]
        end = nc.sbuf_usable_end

        class Area:
            def __init__(self, off):
                self.off = off

            def put(self, name, shape, dt=F32):
                size = 4 if dt != U8 else 1
                for s in shape[1:]:
                    size *= s
                o = self.off
                self.off += size + (-size) % 32
                assert self.off <= end, (name, self.off, end)
                return at(name, shape, dt, o)

        PS = ctx.enter_context(nc.psum_tensor("PS", [128, 8, 512], F32))
        banks = Ring(4)

        def pair():
            i, mark = banks.take()
            PE.wait(mark)
            return i

        def free(i, mark):
            banks.freed[i] = mark

        def flat(i):
            return PS[:, 2 * i:2 * i + 2, :].rearrange("p a b -> p (a b)")

        def f32(x):
            return x.bitcast(F32)

        def cols(x, lo):
            return x[:, 0:T].rearrange("p (a b) -> p a b", a=2) if lo == 0 else x[:, NM:T]

        raw_sem = [slot(f"raw{i}") for i in range(NRAW)]
        n_blocks = DEPTH * BLOCKS_LAYER + BLOCKS_SECOND
        landed, split_done, used = {}, {}, {}
        state = {"load": 0, "split": 0, "use": 0}

        def load_block(after=None):
            j = state["load"]
            if j < n_blocks:
                landed[j] = SP.dma(raw_sem[j % NRAW], RAW[:, j % NRAW, :], d["blocks"][j], after)
                state["load"] += 1

        def split_block():
            j = state["split"]
            if j >= n_blocks:
                return
            hi, lo, raw = WH[:, j % 2, :], WL[:, j % 2, :], RAW[:, j % NRAW, :]
            t = A.op(lambda e: e.activation(hi, raw, ACT.Copy), landed[j], used.get(j - 2))
            t = V.op(lambda e: e.tensor_tensor(lo, raw, f32(hi), ALU.subtract), t)
            split_done[j] = t
            state["split"] += 1
            load_block(t)

        for _ in range(NRAW):
            load_block()

        def block(nk):
            j = state["use"]
            state["use"] += 1
            while state["split"] <= min(j + 1, n_blocks - 1):
                if state["split"] - 2 >= 0 and state["split"] - 2 not in used:
                    break
                split_block()
            PE.wait(split_done[j])
            hi = WH[:, j % 2, :].rearrange("p (k n) -> p k n", k=nk)
            lo = WL[:, j % 2, :].rearrange("p (k n) -> p k n", k=nk)
            return j, hi, lo

        def three(hi_s, lo_s, hi_m, lo_m):
            return ((hi_s, hi_m), (hi_s, lo_m), (lo_s, hi_m))

        def matmul(out, lhsT, rhs, first, last):
            return lambda e: e.matmul(out, lhsT, rhs, start=first, stop=last)

        def product_T(blk, c, nk, mh, ml, lo, ready):
            _, wh, wl = blk
            i = pair()
            PE.wait(ready)
            parts = [(0, 264, 0), (264, 528, 1)] if lo == 0 else [(NM, T, 0)]
            mark = None
            for k in range(nk):
                for n, (s, m) in enumerate(three(wh, wl, mh, ml)):
                    for a, b, bank in parts:
                        fn = matmul(PS[:, 2 * i + bank, 0:b - a], s[:, k, 128 * c:128 * c + 128], m[:, k, a:b],
                                    k == 0 and n == 0, k == nk - 1 and n == 2)
                        if k == nk - 1 and n == 2 and (a, b, bank) == parts[-1]:
                            mark = PE.op(fn)
                        else:
                            PE.quiet(fn)
            view = PS[:, 2 * i:2 * i + 2, 0:264] if lo == 0 else PS[:, 2 * i, 0:512]
            return i, view, mark

        def product_rows(blk, xh, xl, starts, ready):
            _, wh, wl = blk
            i = pair()
            PE.wait(ready)
            mark = None
            for bank, a in enumerate(starts):
                for k in range(8):
                    for n, (s, m) in enumerate(three(xh, xl, wh, wl)):
                        fn = matmul(PS[:, 2 * i + bank, 0:256], s[:, k, a:a + 128], m[:, k, 0:256],
                                    k == 0 and n == 0, k == 7 and n == 2)
                        if k == 7 and n == 2 and bank == len(starts) - 1:
                            mark = PE.op(fn)
                        else:
                            PE.quiet(fn)
            return i, mark

        def split_to(hi, lo, src, ready, free_of=None):
            t = A.op(lambda e: e.activation(hi, src, ACT.Copy), ready, free_of)
            return V.op(lambda e: e.tensor_tensor(lo, src, f32(hi), ALU.subtract), t)

        misc = [0]

        def once(q, out, in_, *marks):
            misc[0] += 1
            return q.dma(slot(f"m{misc[0]}"), out, in_, *marks)

        reused = {}

        def again(name, q, out, in_, *marks):
            if name not in reused:
                reused[name] = slot(name)
            return q.dma(reused[name], out, in_, *marks)

        def root(mean_scale, eps, n, ready):
            t = V.op(lambda e: e.tensor_scalar(SS[:, 0:n], SS[:, 0:n], mean_scale, eps, ALU.mult, ALU.add), ready)
            t = A.op(lambda e: e.activation(RS[:, 0:n], SS[:, 0:n], ACT.Sqrt), t)
            return V.op(lambda e: e.reciprocal(RS[:, 0:n], RS[:, 0:n]), t)

        m_id = once(SP, I128[:, :], d["ident"])
        m_ss = V.op(lambda e: e.memset(SS[:, :], 1.0))
        m_rs = V.op(lambda e: e.memset(RS[:, :], 1.0))
        m_h = [once(SP, HM[:, :], d["meta"])] + \
              [once(SP, H[:, b, :], d["x"][128 * b:128 * b + 128, :]) for b in range(4)]

        def tiles_of(lo):
            out = [(128, H[:, b, :], NM + 128 * b, b) for b in range(4)]
            return out + ([(NM, HM[:, :], 0, 4)] if lo == 0 else [])

        def squares(src, rows, n, junk, ready):
            return A.op(lambda e: e.activation(junk[0:rows, :], src, ACT.Square,
                                               accum_out=SS[0:rows, n:n + 1]), ready)

        def transposed(gain, ready, lo, xt, junk, keep=None, x_free=None):
            marks = [squares(src, rows, n, junk, [ready[n], m_ss, x_free]) for rows, src, _, n in tiles_of(lo)]
            r = root(1.0 / 1024, EPS, 5, marks)
            free_xt = [None, None]
            done = []
            for k, (rows, src, col, n) in enumerate(tiles_of(lo)):
                buf = xt[0:rows, k % 2, :] if keep is None else keep[:, n, :]
                t = V.op(lambda e, buf=buf, src=src, rows=rows, n=n: e.scalar_tensor_tensor(
                    out=buf, in0=src, scalar=RS[0:rows, n:n + 1], in1=GBC[0:rows, :], op0=ALU.mult, op1=ALU.mult),
                    r, gain, free_xt[k % 2], x_free)
                i = pair()
                PE.wait(t, m_id)
                v = flat(i).rearrange("p (k n) -> p k n", k=8)
                for kc in range(8):
                    fn = (lambda e, kc=kc, v=v, buf=buf, rows=rows: e.transpose(
                        v[:, kc, 0:rows], buf[:, 128 * kc:128 * kc + 128], I128[0:rows, 0:rows]))
                    t = PE.op(fn) if kc == 7 else PE.quiet(fn)
                free_xt[k % 2] = t
                t = split_to(XH[:, :, col:col + rows], XL[:, :, col:col + rows], v[:, :, 0:rows], t, x_free)
                free(i, t)
                done.append(t)
            return done

        r0 = Area(r_area)
        YA = r0.put("YA", [128, 8, T])
        YB = r0.put("YB", [128, 8, T])
        c0 = r0.off
        cv = Area(c0)
        CH = cv.put("CH", [128, 8, T], R32)
        CL = cv.put("CL", [128, 8, T], R32)
        UB = cv.put("UB", [128, 2, T + 2])
        HS = cv.put("HS", [128, T])
        ZS = cv.put("ZS", [128, 2, T])
        YC = cv.put("YC", [128, 2, T])
        xa = Area(c0)
        XT = xa.put("XT", [128, 2, 1024])
        JK = xa.put("JK", [128, 1024])
        hd = Area(c0)
        QK = hd.put("QK", [128, 4, T])
        SX = hd.put("SX", [128, 4, 512])
        SM = hd.put("SM", [16, T])
        RPOFF = hd.off
        RP = hd.put("RP", [128, 3, 2, T])
        OO = Area(RPOFF).put("OO", [128, 5, 512])
        CS = hd.put("CS", [128, 2, T])
        RH = hd.put("RH", [128, 4, T], R32)
        hp = Area(h_area)
        VV = hp.put("VV", [128, 5, 512])
        Z = hp.put("Z", [128, 4, T])
        assert hp.off <= r_area
        RL = hd.put("RL", [128, 4, T], R32)
        DX = Area(c0 + 0)
        fn_ = Area(c0)
        YH = fn_.put("YH", [128, 8, T], R32)
        YL = fn_.put("YL", [128, 8, T], R32)
        TG = fn_.put("TG", [128, 2, T])
        y2_at = r_area
        Y2a = Area(r_area)
        Y2 = Y2a.put("Y2", [128, 4, 1024])
        Y2M = Y2a.put("Y2M", [16, 1024])
        JY = Y2a.put("JY", [128, 1024])
        DT = hd.put("DT", [128, 512])
        DM = Area(r_area)
        ST = hd.put("ST", [128, 5, 6])
        MV = hd.put("MV", [128, 5, 2])
        DMT = hd.put("DMT", [16, T])
        BV = hd.put("BV", [128, 512])

        h_store = {}
        ready_h = {b: m_h[b + 1] for b in range(4)}
        ready_h[4] = m_h[0]
        region_free = None
        gbc_free = None
        par_free = None

        for l in range(DEPTH):
            lo = 0 if l + 1 < DEPTH else NM
            m_g = again("gbc", SP, GBC[:, :], d["pre_norm_g"][l].partition_broadcast(128), gbc_free)
            m_bin = again("bin", SP, BIN[:, :], d["b_in_T"][l], par_free)
            m_cw = again("cw", SP, CW[:, :], d["conv_w_T"][l], par_free)
            m_cb = again("cb", SP, CB[:, :], d["conv_b_T"][l], par_free)
            m_gn = again("gng", SP, GNG[:, :], d["gn_g_T"][l], par_free)
            xn = transposed(m_g, ready_h, 0, XT, JK, x_free=region_free)
            parked = h_store.get("marks")

            conv_done = []
            yc_free = [None, None]
            for j in range(8):
                q = j % 2
                b1 = block(8)
                i1, p_h, t_h = product_T(b1, 0, 8, XH, XL, 0, xn)
                i2, p_c, t_c = product_T(b1, 1, 8, XH, XL, 0, None)
                used[b1[0]] = t_c
                b2 = block(8)
                i3, p_b, t_b = product_T(b2, 0, 8, XH, XL, lo, None)
                i4, p_z, t_z = product_T(b2, 1, 8, XH, XL, lo, None)
                used[b2[0]] = t_z
                a1 = A.op(lambda e, p=p_h, j=j: e.activation(cols(HS, 0), p, ACT.Identity, bias=BIN[:, j:j + 1]),
                          t_h, m_bin, conv_done[-1:] or xn)
                free(i1, a1)
                z0 = V.op(lambda e, q=q: e.memset(UB[:, q, 0:2], 0.0), yc_free[q] or xn)
                u = V.op(lambda e, p=p_c, j=j, q=q: e.scalar_tensor_tensor(
                    out=UB[:, q, 2:T + 2].rearrange("p (a b) -> p a b", a=2), in0=p, scalar=BIN[:, 16 + j:17 + j],
                    in1=cols(HS, 0), op0=ALU.add, op1=ALU.mult), t_c, a1)
                free(i2, u)
                a4 = A.op(lambda e, p=p_z, j=j, q=q: e.activation(cols(ZS[:, q, :], lo), p, ACT.Silu,
                                                             bias=BIN[:, 24 + j:25 + j]), t_z, yc_free[q] or xn)
                free(i4, a4)
                y = YC[:, q, lo:T]
                t = V.op(lambda e, y=y, j=j, q=q: e.tensor_scalar(y, UB[:, q, lo:T], CW[:, j:j + 1], CB[:, j:j + 1],
                                                             ALU.mult, ALU.add), u, z0, m_cw, m_cb, yc_free[q])
                for w in (1, 2):
                    t = V.op(lambda e, y=y, j=j, q=q, w=w: e.scalar_tensor_tensor(
                        out=y, in0=UB[:, q, lo + w:T + w], scalar=CW[:, 8 * w + j:8 * w + j + 1], in1=y,
                        op0=ALU.mult, op1=ALU.add), t)
                t = V.op(lambda e, p=p_b, j=j, q=q: e.scalar_tensor_tensor(
                    out=cols(YC[:, q, :], lo), in0=p, scalar=BIN[:, 8 + j:9 + j], in1=cols(YC[:, q, :], lo),
                    op0=ALU.add, op1=ALU.mult), t, t_b)
                free(i3, t)
                t = V.op(lambda e, y=y, q=q: e.tensor_tensor(y, y, ZS[:, q, lo:T], ALU.mult), t, a4)
                t = split_to(CH[:, j, lo:T], CL[:, j, lo:T], y, t)
                yc_free[q] = t
                conv_done.append(t)

            ya = []
            for g in range(4):
                b1 = block(8)
                sg = []
                for c in range(2):
                    j = 2 * g + c
                    i, p, t = product_T(b1, c, 8, XH, XL, lo, None)
                    sg.append(A.op(lambda e, p=p, j=j: e.activation(cols(YA[:, j, :], lo), p, ACT.Sigmoid,
                                                                  bias=BIN[:, 80 + j:81 + j]), t))
                    free(i, sg[-1])
                used[b1[0]] = t
                b2 = block(8)
                for c in range(2):
                    j = 2 * g + c
                    i, p, t = product_T(b2, c, 8, CH, CL, lo, conv_done)
                    v = V.op(lambda e, p=p, j=j: e.tensor_tensor(cols(YA[:, j, :], lo), p, cols(YA[:, j, :], lo),
                                                                 ALU.mult), t, sg[c])
                    free(i, v)
                    ya.append(v)
                used[b2[0]] = t
            conv_used = t

            m_cs = again("cs", SP, CS[:, :, :], d["cos_sin"], conv_used, ya[-1])
            turn = {"qk_free": [conv_used, ya[-1]], "sx_free": [conv_used, ya[-1]], "oo_free": [conv_used, ya[-1]],
                    "vv_free": [parked, ya[-1]], "z_free": [parked, ya[-1]], "rh_free": [conv_used, ya[-1]],
                    "dt_free": [conv_used, ya[-1]], "bv_free": [conv_used, ya[-1]], "st_free": [conv_used, ya[-1]]}
            yb = [None] * 8
            ymarks = []

            def turn_rows(h, norm_done, z_done, m_gn=m_gn, lo=lo, turn=turn):
                marks = []
                for jj in range(0, 4, 2):
                    i = pair()
                    PE.wait(norm_done)
                    for j in (jj, jj + 1):
                        for b in range(4):
                            fn = (lambda e, i=i, j=j, b=b: e.transpose(
                                PS[:, 2 * i + j % 2, 128 * b:128 * b + 128], OO[:, b, 128 * j:128 * j + 128], I128[:, :]))
                            t = PE.op(fn) if b == 3 and j % 2 else PE.quiet(fn)
                    for j in (jj, jj + 1):
                        v = V.op(lambda e, i=i, j=j, h=h: e.scalar_tensor_tensor(
                            out=Z[:, j, NM:T], in0=PS[:, 2 * i + j % 2, :], scalar=GNG[:, 4 * h + j:4 * h + j + 1],
                            in1=Z[:, j, NM:T], op0=ALU.mult, op1=ALU.mult), t, z_done, m_gn)
                        marks.append(v)
                    free(i, v)
                if lo == 0:
                    i = pair()
                    for j in range(4):
                        fn = (lambda e, i=i, j=j: e.transpose(
                            PS[:, 2 * i, NM * j:NM * j + NM], OO[0:NM, 4, 128 * j:128 * j + 128], I128[0:NM, 0:NM]))
                        t = PE.op(fn) if j == 3 else PE.quiet(fn)
                    for j in range(4):
                        v = V.op(lambda e, i=i, j=j, h=h: e.scalar_tensor_tensor(
                            out=Z[:, j, 0:NM], in0=PS[:, 2 * i, NM * j:NM * j + NM],
                            scalar=GNG[:, 4 * h + j:4 * h + j + 1], in1=Z[:, j, 0:NM], op0=ALU.mult, op1=ALU.mult), t)
                        marks.append(v)
                    free(i, v)
                turn["oo_free"] = [t]
                out = split_to(RH[:, :, lo:T], RL[:, :, lo:T], Z[:, :, lo:T], marks, turn["rh_free"])
                turn["z_free"] = [out]
                return out

            def out_rows(h, ret_done, lo=lo, turn=turn, yb=yb):
                for half in range(2):
                    blk = block(4)
                    for c in range(4):
                        j = 4 * half + c
                        i, p, t = product_T(blk, c, 4, RH, RL, lo, ret_done)
                        if h == 0:
                            v = A.op(lambda e, p=p, j=j: e.activation(cols(YB[:, j, :], lo), p, ACT.Copy), t)
                        else:
                            v = V.op(lambda e, p=p, j=j: e.tensor_tensor(cols(YB[:, j, :], lo), p,
                                                                         cols(YB[:, j, :], lo), ALU.add), t, yb[j])
                        free(i, v)
                        yb[j] = v
                    used[blk[0]] = t
                turn["rh_free"] = [t]

            before = None
            for h in range(5):
                if h < 4:
                    m_dt = again("dt", SP, DT[:, :], d["decay"][h], turn["dt_free"])
                    m_dm = again("dm", SP, DMT[:, :], d["decay_meta"][h], turn["dt_free"])
                    m_bv = again("bv", SP, BV[:, :], d["b_in"][l, 6144 + 512 * h:6656 + 512 * h].partition_broadcast(128),
                                 turn["bv_free"])
                    qk = []
                    for n in range(2):
                        blk = block(8)
                        for c in range(2):
                            i, p, t = product_T(blk, c, 8, XH, XL, 0, None)
                            col = 32 + 8 * n + 2 * h + c
                            a = A.op(lambda e, p=p, n=n, c=c, col=col: e.activation(
                                cols(QK[:, 2 * n + c, :], 0), p, ACT.Identity, bias=BIN[:, col:col + 1]),
                                t, turn["qk_free"])
                            free(i, a)
                            qk.append(a)
                        used[blk[0]] = t
                if before is not None:
                    ret_done = turn_rows(h - 1, *before)
                if h < 4:
                    one, two = QK[:, 0:4:2, :], QK[:, 1:4:2, :]

                    def table(n):
                        return CS[:, n, :].unsqueeze(1).broadcast_to([128, 2, T])
                    a1 = V.op(lambda e: e.tensor_tensor(RP[:, 0], one, table(0), ALU.mult), qk, m_cs, turn["oo_free"])
                    a2 = V.op(lambda e: e.tensor_tensor(RP[:, 1], two, table(1), ALU.mult))
                    a3 = V.op(lambda e: e.tensor_tensor(RP[:, 2], one, table(1), ALU.mult))
                    a4 = V.op(lambda e: e.tensor_tensor(one, RP[:, 0], RP[:, 1], ALU.subtract), a2, a3)
                    a5 = V.op(lambda e: e.tensor_tensor(RP[:, 0], two, table(0), ALU.mult), a4)
                    rot = V.op(lambda e: e.tensor_tensor(two, RP[:, 2], RP[:, 0], ALU.add), a5)
                    vm = []
                    for n in range(2):
                        blk = block(8)
                        for b in (0, 2):
                            i, t = product_rows(blk, XH, XL, [NM + 128 * b, NM + 128 * b + 128], None)
                            v = V.op(lambda e, i=i, b=b, n=n: e.tensor_tensor(
                                VV[:, b:b + 2, 256 * n:256 * n + 256], PS[:, 2 * i:2 * i + 2, 0:256],
                                BV[:, 256 * n:256 * n + 256].unsqueeze(1).broadcast_to([128, 2, 256]), ALU.add),
                                t, m_bv, turn["vv_free"])
                            free(i, v)
                            vm.append(v)
                        i, t = product_rows(blk, XH, XL, [0], None)
                        v = V.op(lambda e, i=i, n=n: e.tensor_tensor(
                            VV[0:NM, 4, 256 * n:256 * n + 256], PS[0:NM, 2 * i, 0:256],
                            BV[0:NM, 256 * n:256 * n + 256], ALU.add), t)
                        free(i, v)
                        vm.append(v)
                        used[blk[0]] = t
                    turn["bv_free"] = [v]
                if before is not None:
                    out_rows(h - 1, ret_done)
                if h == 4:
                    break
                sm = []
                for mb in range(0, 4, 2):
                    i = pair()
                    PE.wait(rot)
                    for m in (mb, mb + 1):
                        a = NM + 128 * m
                        for dk in range(2):
                            fn = matmul(PS[:, 2 * i + m % 2, 0:T - a], QK[:, 2 + dk, a:a + 128], QK[:, dk, a:T],
                                        dk == 0, dk == 1)
                            t = PE.op(fn) if dk and m % 2 else PE.quiet(fn)
                    for m in (mb, mb + 1):
                        n = 512 - 128 * m
                        v = V.op(lambda e, i=i, m=m, n=n: e.tensor_tensor(SX[:, m, 0:n], PS[:, 2 * i + m % 2, 0:n],
                                                                        DT[:, 0:n], ALU.mult), t, m_dt, turn["sx_free"])
                        sm.append(v)
                    free(i, v)
                i = pair()
                qs = [(NM, T, 1)] + ([(0, NM, 0)] if lo == 0 else [])
                for a, b, bank in qs:
                    for dk in range(2):
                        fn = matmul(PS[0:NM, 2 * i + bank, 0:b - a], QK[:, 2 + dk, 0:NM], QK[:, dk, a:b],
                                    dk == 0, dk == 1)
                        t = PE.op(fn) if dk and bank == qs[-1][2] else PE.quiet(fn)
                turn["qk_free"] = [t]
                for a, b, bank in qs:
                    v = V.op(lambda e, i=i, a=a, b=b, bank=bank: e.tensor_tensor(
                        SM[:, a:b], PS[0:NM, 2 * i + bank, 0:b - a], DMT[:, a:b], ALU.mult), t, m_dm, turn["sx_free"])
                    sm.append(v)
                free(i, v)
                turn["dt_free"] = [v]
                zm = []
                for n in range(2):
                    blk = block(8)
                    for c in range(2):
                        j = 2 * n + c
                        i, p, t = product_T(blk, c, 8, XH, XL, lo, None)
                        col = 64 + 4 * h + j
                        a = A.op(lambda e, p=p, j=j, col=col: e.activation(cols(Z[:, j, :], lo), p, ACT.Silu,
                                                                          bias=BIN[:, col:col + 1]),
                                 t, m_bin, turn["z_free"])
                        free(i, a)
                        zm.append(a)
                    used[blk[0]] = t
                om = []
                todo = [0, 1, 2, 3] + ([4] if lo == 0 else [])
                for n0 in range(0, len(todo), 2):
                    i = pair()
                    PE.wait(sm, vm)
                    for b in todo[n0:n0 + 2]:
                        bank = 2 * i + b % 2
                        if b == 4:
                            t = PE.op(matmul(PS[0:NM, bank, :], SM[:, 0:NM], VV[0:NM, 4, :], True, True))
                            continue
                        for m in range(b + 1):
                            PE.quiet(matmul(PS[:, bank, :], SX[:, m, 128 * (b - m):128 * (b - m) + 128],
                                            VV[:, m, :], m == 0, False))
                        t = PE.op(matmul(PS[:, bank, :], SM[:, NM + 128 * b:NM + 128 * b + 128], VV[0:NM, 4, :],
                                         False, True))
                    for b in todo[n0:n0 + 2]:
                        rows = NM if b == 4 else 128
                        a = A.op(lambda e, i=i, b=b, rows=rows: e.activation(
                            OO[0:rows, b, :], PS[0:rows, 2 * i + b % 2, :], ACT.Copy), t, rot, turn["oo_free"])
                        om.append((rows, b, a))
                    free(i, a)
                turn["vv_free"] = [t]
                turn["sx_free"] = [t]
                norm = []
                for rows, b, a in om:
                    v = V.op(lambda e, rows=rows, b=b: e.bn_stats(ST[0:rows, b, :], OO[0:rows, b, :]), a, turn["st_free"])
                    v = V.op(lambda e, rows=rows, b=b: e.bn_aggr(MV[0:rows, b, :], ST[0:rows, b, :]), v)
                    norm.append(V.op(lambda e, rows=rows, b=b: e.tensor_copy(SS[0:rows, b:b + 1], MV[0:rows, b, 1:2]), v))
                r = root(1.0, GN_EPS, 5, norm)
                nd = []
                for rows, b, a in om:
                    nd.append(V.op(lambda e, rows=rows, b=b: e.tensor_scalar(
                        OO[0:rows, b, :], OO[0:rows, b, :], MV[0:rows, b, 0:1], RS[0:rows, b:b + 1],
                        ALU.subtract, ALU.mult), r))
                turn["st_free"] = [nd[-1]]
                before = (nd, zm)

            ym = []
            tg_free = [None, None]
            heads_end = [t_ for t_ in turn["rh_free"]] + [yb[-1]]
            for g in range(4):
                blk = block(8)
                for c in range(2):
                    j = 2 * g + c
                    i, p, t = product_T(blk, c, 8, XH, XL, lo, None)
                    a = A.op(lambda e, p=p, j=j, c=c: e.activation(cols(TG[:, c, :], lo), p, ACT.Sigmoid,
                                                                 bias=BIN[:, 88 + j:89 + j]), t, tg_free[c], heads_end)
                    free(i, a)
                    y = TG[:, c, lo:T]
                    v = V.op(lambda e, y=y, j=j: e.tensor_tensor(y, y, YB[:, j, lo:T], ALU.mult), a, yb[j])
                    v = V.op(lambda e, y=y, j=j: e.tensor_tensor(y, y, YA[:, j, lo:T], ALU.add), v, ya[j])
                    v = split_to(YH[:, j, lo:T], YL[:, j, lo:T], y, v, heads_end)
                    tg_free[c] = v
                    ym.append(v)
                used[blk[0]] = t
            region_free = t
            par_free = a
            src = d["x"] if l == 0 else d["hx"]
            back = [again(f"hb{b}", SP, H[:, b, :], src[128 * b:128 * b + 128, :], turn["vv_free"], turn["z_free"])
                    for b in range(4)]
            if lo == 0:
                back.append(again("hb4", SP, HM[:, :], d["meta"], turn["vv_free"], turn["z_free"]))
            m_g = again("gbc", SP, GBC[:, :], d["post_norm_g"][l].partition_broadcast(128), xn)
            y2 = {b: [] for b in range(5)}
            for n in range(4):
                blk = block(8)
                for b in (0, 2):
                    i, t = product_rows(blk, YH, YL, [NM + 128 * b, NM + 128 * b + 128], ym)
                    a = A.op(lambda e, i=i, b=b, n=n: e.activation(Y2[:, b:b + 2, 256 * n:256 * n + 256],
                                                                 PS[:, 2 * i:2 * i + 2, 0:256], ACT.Copy), t)
                    free(i, a)
                    y2[b].append(a)
                    y2[b + 1].append(a)
                if lo == 0:
                    i, t = product_rows(blk, YH, YL, [0], None)
                    a = A.op(lambda e, i=i, n=n: e.activation(Y2M[:, 256 * n:256 * n + 256], PS[0:NM, 2 * i, 0:256],
                                                            ACT.Copy), t)
                    free(i, a)
                    y2[4].append(a)
                used[blk[0]] = t
            y_used = t
            rows_of = [(128, Y2[:, b, :], H[:, b, :], b) for b in range(4)]
            if lo == 0:
                rows_of.append((NM, Y2M[:, :], HM[:, :], 4))
            sq = [squares(y, rows, b, JY, y2[b]) for rows, y, _, b in rows_of]
            r = root(1.0 / 1024, EPS, 5, sq)
            ready_h = {}
            stores = []
            for rows, y, h_, b in rows_of:
                v = V.op(lambda e, rows=rows, y=y, b=b: e.scalar_tensor_tensor(
                    out=y, in0=y, scalar=RS[0:rows, b:b + 1], in1=GBC[0:rows, :], op0=ALU.mult, op1=ALU.mult), r, m_g)
                gbc_free = v
                v = V.op(lambda e, y=y, h_=h_: e.tensor_tensor(h_, h_, y, ALU.add), v, back[b])
                ready_h[b] = v
                if b < 4:
                    stores.append(again(f"hs{b}", SP, d["hx"][128 * b:128 * b + 128, :], h_, v, back[b]))
            h_store["marks"] = stores
            region_free = [region_free, y_used, v]

        m_g = again("gbc", SP, GBC[:, :], d["norm1_g_2"][0].partition_broadcast(128), gbc_free)
        sa = Area(r_area)
        XT2 = sa.put("XT2", [128, 2, 1024])
        JK2 = sa.put("JK2", [128, 1024])
        x2_end = [None]
        xn = transposed(m_g, ready_h, NM, XT2, JK2, x_free=region_free)
        sa = Area(h_area)
        V2 = sa.put("V2", [128, 4, 1024])
        GH = sa.put("GH", [128, 6, 2])
        sa = Area(r_area)
        Q6 = sa.put("Q6", [128, 6, 512])
        K6 = sa.put("K6", [128, 6, 512])
        F6 = sa.put("F6", [128, 6, 512])
        G6 = sa.put("G6", [128, 6, 512])
        GT = sa.put("GT", [128, 8, 512])
        SD = sa.put("SD", [128, 8, 512])
        MK = sa.put("MK", [128, 8, 128])
        WGL = Area(h_area + 16640).put("WGL", [128, 8, 16])
        small = Area(h_area + 16640 + 512)
        GLT = small.put("GLT", [16, 512])
        UPW = small.put("UPW", [16, 256])
        assert small.off <= r_area, (small.off, r_area)
        ga_ = Area(r_area)
        so_ = Area(x_area)
        SO = so_.put("SO", [128, 8, 6, 128])
        BG = at("BG", [128, 2], F32, area(0)) if False else LGT

        parked = h_store["marks"]
        m_mk = once(SP, MK[:, :, :], d["masks"], xn)
        m_wgl = once(SP, WGL[:, :, :], d["w_glow"], xn, parked)
        m_upw = once(SP, UPW[:, :], d["gla_w_gate_up_2"][0], xn, parked)
        m_lgt = once(SP, LGT[:, :], d["logits_T"])
        m_vg = once(SP, VG[:, :], d["small_T"])
        sd0 = V.op(lambda e: e.memset(SD[:, :, :], 0.0), xn)

        l0, l1 = LGT[:, 0:4], LGT[:, 4:8]
        B = [LBS[:, n, :] for n in range(6)]
        t = V.op(lambda e: e.tensor_tensor(B[0], l0, l1, ALU.max), m_lgt)
        t = V.op(lambda e: e.tensor_tensor(B[1], l0, B[0], ALU.subtract), t)
        t1 = V.op(lambda e: e.tensor_tensor(B[2], l1, B[0], ALU.subtract), t)
        t = A.op(lambda e: e.activation(B[3], B[1], ACT.Exp), t, t1)
        t = A.op(lambda e: e.activation(B[4], B[2], ACT.Exp), t)
        t = V.op(lambda e: e.tensor_tensor(B[5], B[3], B[4], ALU.add), t)
        t = V.op(lambda e: e.reciprocal(B[0], B[5]), t)
        t = V.op(lambda e: e.tensor_tensor(B[1], B[3], B[0], ALU.mult), t)
        m_lb = V.op(lambda e: e.tensor_scalar(B[2], B[1], -1.0, 1.0, ALU.mult, ALU.add), t)
        LB, LB1 = B[1], B[2]

        def tile512(blk, c, fn_evac):
            i, p, t = product_T(blk, c, 8, XH, XL, NM, xn)
            m = fn_evac(p, t)
            free(i, m)
            return m, t

        i = pair()
        PE.wait(xn, m_wgl, m_upw)
        for k in range(8):
            for n, part in enumerate((XH, XL)):
                PE.quiet(matmul(PS[0:16, 2 * i, :], WGL[:, k, :], f32(part[:, k, NM:T]), k == 0 and n == 0,
                                k == 7 and n == 1)) if not (k == 7 and n == 1) else None
        t = PE.op(matmul(PS[0:16, 2 * i, :], WGL[:, 7, :], f32(XL[:, 7, NM:T]), False, True))
        a = A.op(lambda e, i=i: e.activation(GLT[:, :], PS[0:16, 2 * i, :], ACT.Copy), t, parked)
        free(i, a)
        i = pair()
        PE.wait(a)
        PE.quiet(matmul(PS[:, 2 * i, :], UPW[:, 0:128], GLT[:, :], True, True))
        t = PE.op(matmul(PS[:, 2 * i + 1, :], UPW[:, 128:256], GLT[:, :], True, True))
        gz = F6[:, 4:6, :]
        tmp = G6[:, 4:6, :]
        gt2 = G6[:, 2:4, :]
        for c in range(2):
            a = A.op(lambda e, i=i, c=c: e.activation(F6[:, 4 + c, :], PS[:, 2 * i + c, :], ACT.Identity,
                                                    bias=VG[:, 2 + c:3 + c]), t, m_vg, xn)
        free(i, a)
        t = A.op(lambda e: e.activation(tmp, gz, ACT.Abs), a)
        t = A.op(lambda e: e.activation(tmp, tmp, ACT.Exp, scale=-1.0), t)
        t = V.op(lambda e: e.tensor_scalar(tmp, tmp, 1.0, None, ALU.add), t)
        t = A.op(lambda e: e.activation(gt2, tmp, ACT.Ln), t)
        t = V.op(lambda e: e.scalar_tensor_tensor(out=tmp, in0=gz, scalar=0.0, in1=gt2, op0=ALU.min,
                                                  op1=ALU.subtract), t)
        m_fg = A.op(lambda e: e.activation(gz, tmp, ACT.Exp, scale=1.0 / 16), t)

        qm, km, fm = [None] * 6, [None] * 6, [None] * 6
        fm[4] = fm[5] = m_fg
        for g in range(2):
            blk = block(8)
            for c in range(2):
                n = 2 * g + c
                qm[n], t = tile512(blk, c, lambda p, t, n=n: A.op(
                    lambda e: e.activation(Q6[:, n, :], p, ACT.Silu), t))
            used[blk[0]] = t
        for g in range(2):
            blk = block(8)
            for c in range(2):
                n = 2 * g + c
                s, t = tile512(blk, c, lambda p, t, n=n: A.op(
                    lambda e: e.activation(F6[:, n, :], p, ACT.Sigmoid), t))
                fm[n] = V.op(lambda e, n=n: e.tensor_scalar(F6[:, n, :], F6[:, n, :], LB1[:, n:n + 1], LB[:, n:n + 1],
                                                          ALU.mult, ALU.add), s, m_lb)
                km[n] = V.op(lambda e, n=n: e.tensor_scalar(K6[:, n, :], F6[:, n, :], -1.0, 1.0, ALU.mult, ALU.add),
                             fm[n])
            used[blk[0]] = t
        blk = block(8)
        for c in range(2):
            qm[4 + c], t = tile512(blk, c, lambda p, t, c=c: A.op(
                lambda e: e.activation(Q6[:, 4 + c, :], p, ACT.Copy, scale=0.125), t))
        used[blk[0]] = t
        blk = block(8)
        for c in range(2):
            km[4 + c], t = tile512(blk, c, lambda p, t, c=c: A.op(
                lambda e: e.activation(K6[:, 4 + c, :], p, ACT.Copy), t))
        used[blk[0]] = t

        vmarks, gmarks = [], [None] * 8

        def rest():
            for g in range(4):
                blk = block(8)
                for b in (0, 2):
                    i, t = product_rows(blk, XH, XL, [NM + 128 * b, NM + 128 * b + 128], None)
                    a = A.op(lambda e, i=i, b=b, g=g: e.activation(V2[:, b:b + 2, 256 * g:256 * g + 256],
                                                                 PS[:, 2 * i:2 * i + 2, 0:256], ACT.Copy), t, parked)
                    free(i, a)
                    vmarks.append(a)
                    if b == 2:
                        used[blk[0]] = t
                    yield t
            for g in range(4):
                blk = block(8)
                for c in range(2):
                    j = 2 * g + c
                    gmarks[j], t = tile512(blk, c, lambda p, t, j=j: A.op(
                        lambda e: e.activation(GT[:, j, :], p, ACT.Silu), t))
                    if c == 1:
                        used[blk[0]] = t
                    yield t

        side = rest()
        last_side = [None]

        def step_side(n=1):
            for _ in range(n):
                t = next(side, None)
                if t is not None:
                    last_side[0] = t

        heads_of = [[n] for n in range(4)] + [[4, 5], [6, 7]]
        sdm = [sd0] * 8
        som = [[] for _ in range(8)]

        def score(grp, pieces, evac):
            marks = []
            for hh in heads_of[grp]:
                i = pair()
                rows = slice(0, 128) if grp < 4 else slice(64 * (hh % 2), 64 * (hh % 2) + 64)
                PE.wait(qm[grp], km[grp])
                for n, (col, (k0, k1), (q0, q1)) in enumerate(pieces):
                    fn = matmul(PS[:, 2 * i, col:col + q1 - q0], K6[rows, grp, k0:k1], Q6[rows, grp, q0:q1], True, True)
                    t = PE.op(fn) if n == len(pieces) - 1 else PE.quiet(fn)
                free(i, evac(hh, i, t))
                marks.append(t)
            return marks

        def masked(level):
            def evac(hh, i, t):
                sdm[hh] = V.op(lambda e: e.copy_predicated(
                    SD[:, hh, :].rearrange("p (b q) -> p b q", b=4),
                    MK[:, level, :].bitcast(U32).unsqueeze(1).broadcast_to([128, 4, 128]),
                    PS[:, 2 * i, :].rearrange("p (b q) -> p b q", b=4)), t, m_mk, sdm[hh])
                return sdm[hh]
            return evac

        diag = [(128 * b, (128 * b, 128 * b + 128), (128 * b, 128 * b + 128)) for b in range(4)]
        for grp in range(6):
            done = score(grp, diag, masked(0))
            qm[grp] = V.op(lambda e, grp=grp: e.tensor_tensor(Q6[:, grp, :], Q6[:, grp, :], F6[:, grp, :], ALU.mult),
                           done, fm[grp], qm[grp])
        tot = F6
        off = 0
        tm = list(fm)
        goff = 0
        for lv in range(9):
            s = 1 << lv
            if s == 128:
                step_side(99)
            for grp in range(6):
                if s <= 64:
                    done = score(grp, diag, masked(lv + 1))
                else:
                    if s == 128:
                        pieces = [(0, (0, 128), (128, 256)), (128, (256, 384), (384, 512))]
                        span, o0 = 256, 0
                    else:
                        pieces = [(0, (0, 128), (256, 512)), (256, (128, 256), (256, 512))]
                        span, o0 = 512, 2

                    def evac(hh, i, t, span=span, o0=o0):
                        m = A.op(lambda e: e.activation(
                            SO[:, hh, o0:o0 + span // 128, :].rearrange("p a b -> p (a b)"), PS[:, 2 * i, 0:span],
                            ACT.Copy), t, last_side[0])
                        som[hh].append(m)
                        return m
                    done = score(grp, pieces, evac)
                if s < 256:
                    n = 512 // s
                    if s == 1:
                        tv = F6[:, grp, :]
                    else:
                        tv = G6[:, grp, goff:goff + n]
                    tv = tv.rearrange("p (c two) -> p c two", two=2)
                    nxt = 0 if s == 1 else goff + n
                    q4 = Q6[:, grp, :].rearrange("p (c two s) -> p c two s", two=2, s=s)[:, :, 1, :]
                    k4 = K6[:, grp, :].rearrange("p (c two s) -> p c two s", two=2, s=s)[:, :, 0, :]
                    left = tv[:, :, 0:1].broadcast_to([128, n // 2, s])
                    right = tv[:, :, 1:2].broadcast_to([128, n // 2, s])
                    qm[grp] = V.op(lambda e, q4=q4, left=left: e.tensor_tensor(q4, q4, left, ALU.mult),
                                   done, tm[grp], qm[grp])
                    km[grp] = V.op(lambda e, k4=k4, right=right: e.tensor_tensor(k4, k4, right, ALU.mult), km[grp])
                    tm[grp] = V.op(lambda e, tv=tv, grp=grp, nxt=nxt, n=n: e.tensor_tensor(
                        G6[:, grp, nxt:nxt + n // 2], tv[:, :, 0], tv[:, :, 1], ALU.mult), m_fg)
                if (grp + 6 * lv) % 2 == 0:
                    step_side()
            goff = 0 if s == 1 else goff + 512 // s
        step_side(99)
        levels_used = done

        mh_ = Area(r_area)
        MH = mh_.put("MH", [128, 8, 512], R32)
        ML = mh_.put("ML", [128, 8, 512], R32)
        OT = mh_.put("OT", [128, 1024])
        assert mh_.off <= r_area + 4 * 12288
        SQ = at("SQ", [128, 1024], F32, mh_.off)
        mixed = []
        scaled_free = None
        sq_free = None
        for b in range(4):
            i = pair()
            PE.wait(sdm, som[0], som[1], som[2], som[3], som[4], som[5], som[6], som[7], vmarks)
            for hh in range(8):
                for m in range(b + 1):
                    if m == b:
                        st = SD[:, hh, 128 * b:128 * b + 128]
                    elif (m, b) in ((0, 1), (2, 3)):
                        st = SO[:, hh, m // 2, :]
                    else:
                        st = SO[:, hh, 2 + 2 * m + b - 2, :]
                    fn = matmul(flat(i)[:, 128 * hh:128 * hh + 128], st, V2[:, m, 128 * hh:128 * hh + 128],
                                m == 0, m == b)
                    t = PE.op(fn) if hh == 7 and m == b else PE.quiet(fn)
            v_used = t
            a = A.op(lambda e, i=i: e.activation(SQ[:, :], flat(i), ACT.Square), t, sq_free, levels_used)
            v = V.op(lambda e: e.tensor_reduce(SS[:, :], SQ[:, :].rearrange("p (h v) -> p h v", h=8), AX.X, ALU.add), a)
            sq_free = v
            r = root(1.0 / 128, EPS, 8, v)
            v = V.op(lambda e, i=i: e.tensor_tensor(
                OT[:, :].rearrange("p (h v) -> p h v", h=8), flat(i).rearrange("p (h v) -> p h v", h=8),
                RS[:, :].unsqueeze(2).broadcast_to([128, 8, 128]), ALU.mult), r, scaled_free)
            free(i, v)
            i = pair()
            PE.wait(v)
            for j in range(8):
                fn = lambda e, i=i, j=j: e.transpose(flat(i)[:, 128 * j:128 * j + 128],
                                                     OT[:, 128 * j:128 * j + 128], I128[:, :])
                t = PE.op(fn) if j == 7 else PE.quiet(fn)
            scaled_free = t
            vs = []
            for half in range(2):
                gv = GT[:, 4 * half:4 * half + 4, 128 * b:128 * b + 128]
                vs.append(V.op(lambda e, i=i, half=half, gv=gv: e.scalar_tensor_tensor(
                    out=gv, in0=PS[:, 2 * i + half, :].rearrange("p (j q) -> p j q", j=4),
                    scalar=VG[:, half:half + 1], in1=gv, op0=ALU.mult, op1=ALU.mult), t, gmarks, m_vg))
            free(i, vs[-1])
            gv = GT[:, :, 128 * b:128 * b + 128]
            mixed.append(split_to(MH[:, :, 128 * b:128 * b + 128], ML[:, :, 128 * b:128 * b + 128], gv, vs,
                                  levels_used))
        back = [again(f"hb{b}", SP, H[:, b, :], d["hx"][128 * b:128 * b + 128, :], v_used, m_fg) for b in range(4)]
        m_g = again("gbc", SP, GBC[:, :], d["norm2_g_2"][0].partition_broadcast(128), xn)
        hm = {b: back[b] for b in range(4)}
        for n in range(4):
            blk = block(8)
            for b in (0, 2):
                i, t = product_rows(blk, MH, ML, [128 * b, 128 * b + 128], mixed)
                hv = H[:, b:b + 2, 256 * n:256 * n + 256]
                v = V.op(lambda e, i=i, hv=hv: e.tensor_tensor(hv, hv, PS[:, 2 * i:2 * i + 2, 0:256], ALU.add),
                         t, hm[b], hm[b + 1])
                free(i, v)
                hm[b] = hm[b + 1] = v
            used[blk[0]] = t
        out_used = t

        pa = Area(r_area)
        HN = pa.put("HN", [128, 4, 1024])
        QP = pa.put("QP", [128, 16, 512])
        KT = pa.put("KT", [128, 16, 128])
        SC = pa.put("SC", [128, 16, 128])
        CN = SC
        EQ = pa.put("EQ", [128, 2048])
        TV = pa.put("TV", [128, 16, 16])
        TI = pa.put("TI", [128, 16, 16], U32)
        TF = pa.put("TF", [128, 16, 16])
        BV8 = pa.put("BV8", [128, 8, 16])
        BP = pa.put("BP", [128, 8, 16], U32)
        BI = pa.put("BI", [128, 2, 128], U32)
        BF = pa.put("BF", [128, 2, 128])
        EF = pa.put("EF", [128, 2, 128])
        IO = pa.put("IO", [128, 16])
        IDX = pa.put("IDX", [128, 2, 128], U32)
        GW = pa.put("GW", [128, 2, 128])
        AC = pa.put("AC", [128, 2, 128])
        AG = pa.put("AG", [128, 2, 128])
        SW = pa.put("SW", [128, 8, 4])
        DG = pa.put("DG", [128, 8, 128])
        JP = at("JP", [128, 1024], F32, r_area + 16384)
        US = at("US", [128, 2 * NSLOT, 1024], F32, w_area)
        assert w_area + 2 * NSLOT * 4096 <= x_area + 2 * 16896

        m_kt = once(SP, KT[:, :, :], d["keys_T"], out_used, mixed)
        m_io = once(SP, IO[:, :], d["iota"].partition_broadcast(128), out_used, mixed)
        xn2 = transposed(m_g, {b: [hm[b], out_used] + mixed for b in range(4)}, NM, None, JP, keep=HN,
                         x_free=v_used)
        m_g = again("gbc", SP, GBC[:, :], d["norm_f_g_2"].partition_broadcast(128), xn2)
        qpm = []
        for g in range(8):
            blk = block(8)
            for c in range(2):
                j = 2 * g + c
                i, p, t = product_T(blk, c, 8, XH, XL, NM, xn2)
                a = A.op(lambda e, p=p, j=j: e.activation(QP[:, j, :], p, ACT.Copy), t, xn2)
                free(i, a)
                qpm.append(a)
            used[blk[0]] = t
        q_used = t

        tile_free = {0: None, 1: None}
        routed = {}
        sc_free = [None]

        def route(b):
            par = b % 2
            sc = []
            for half in range(2):
                i = pair()
                PE.wait(qpm, m_kt)
                for n in range(8):
                    hp_ = 8 * half + n
                    fn = matmul(flat(i)[:, 128 * n:128 * n + 128], QP[:, hp_, 128 * b:128 * b + 128], KT[:, hp_, :],
                                True, True)
                    t = PE.op(fn) if n == 7 else PE.quiet(fn)
                a = A.op(lambda e, i=i, half=half: e.activation(
                    SC[:, 8 * half:8 * half + 8, :].rearrange("p a b -> p (a b)"), flat(i), ACT.Copy), t, sc_free[0])
                free(i, a)
                sc.append(a)
            yield

            def top16(src, vals, idx, ready):
                a1 = V.op(lambda e: e.max(vals[:, 0:8], src), ready)
                a2 = V.op(lambda e: e.max_index(idx[:, 0:8], vals[:, 0:8], src), a1)
                a3 = V.op(lambda e: e.match_replace(src, vals[:, 0:8], src, LOWEST), a2)
                a4 = V.op(lambda e: e.max(vals[:, 8:16], src), a3)
                return V.op(lambda e: e.max_index(idx[:, 8:16], vals[:, 8:16], src), a4)

            for hp_ in range(16):
                t = top16(SC[:, hp_, :], TV[:, hp_, :], TI[:, hp_, :], sc)
                if hp_ % 2:
                    yield
            tf = V.op(lambda e: e.tensor_copy(TF[:, :, :], TI[:, :, :]), t)
            cand = CN[:, :, :].rearrange("p (h two) n -> p h (two n)", two=2)
            tv = TV[:, :, :].rearrange("p (h two) n -> p h two n", two=2)
            tfv = TF[:, :, :].rearrange("p (h two) n -> p h two n", two=2)
            t = V.op(lambda e: e.tensor_tensor(
                cand.rearrange("p h (i j) -> p h i j", i=16),
                tv[:, :, 0, :].unsqueeze(3).broadcast_to([128, 8, 16, 16]),
                tv[:, :, 1, :].unsqueeze(2).broadcast_to([128, 8, 16, 16]), ALU.add), t)
            yield
            for h in range(8):
                t = top16(cand[:, h, :], BV8[:, h, :], BP[:, h, :], t)
                yield
            sc_free[0] = t
            bp = BP[:, :, :].rearrange("p h k -> p (h k)")
            t = V.op(lambda e: e.tensor_scalar(BI[:, 0, :], bp, 4, None, ALU.logical_shift_right), t)
            t = V.op(lambda e: e.tensor_scalar(BI[:, 1, :], bp, 15, None, ALU.bitwise_and), t)
            t = V.op(lambda e: e.tensor_copy(BF[:, :, :], BI[:, :, :]), t)
            for n in range(2):
                eq = EQ[:, :].rearrange("p (h k a) -> p h k a", h=8, k=16)
                flat_eq = EQ[:, :].rearrange("p (hk a) -> p hk a", a=16)
                t = V.op(lambda e, n=n: e.tensor_tensor(
                    flat_eq, BF[:, n, :].unsqueeze(2).broadcast_to([128, 128, 16]),
                    IO[:, :].unsqueeze(1).broadcast_to([128, 128, 16]), ALU.is_equal), t, m_io)
                t = V.op(lambda e, n=n: e.tensor_tensor(
                    eq, eq, tfv[:, :, n, :].unsqueeze(2).broadcast_to([128, 8, 16, 16]), ALU.mult), t, tf)
                t = V.op(lambda e, n=n: e.tensor_reduce(EF[:, n, :], flat_eq, AX.X, ALU.add), t)
                yield
            t = V.op(lambda e: e.scalar_tensor_tensor(out=EF[:, 0, :], in0=EF[:, 0, :], scalar=128.0,
                                                      in1=EF[:, 1, :], op0=ALU.mult, op1=ALU.add), t)
            idx = V.op(lambda e: e.tensor_copy(IDX[:, par, :], EF[:, 0, :]), t, tile_free[par])
            yield
            gw = GW[:, par, :].rearrange("p (h k) -> p h k", h=8)
            t = V.op(lambda e: e.tensor_tensor(gw, BV8[:, :, :], BV8[:, :, 0:1].broadcast_to([128, 8, 16]),
                                               ALU.subtract), idx)
            t = A.op(lambda e: e.activation(GW[:, par, :], GW[:, par, :], ACT.Exp), t)
            t = V.op(lambda e: e.tensor_reduce(SW[:, :, 0], gw, AX.X, ALU.add), t)
            t = V.op(lambda e: e.reciprocal(SW[:, :, 1], SW[:, :, 0]), t)
            t = V.op(lambda e: e.tensor_tensor(gw, gw, SW[:, :, 1:2].broadcast_to([128, 8, 16]), ALU.mult), t)
            routed[b] = (idx, t)
            yield

        for _ in route(0):
            pass

        g_sem = [slot(f"g{n}") for n in range(2 * NSLOT)]
        ring_free = [[q_used, list(split_done.values())[-1], out_used]] * (2 * NSLOT)
        ring_at = [0, 0]

        def gather(kind, b, n):
            s = NSLOT * kind + ring_at[kind] % NSLOT
            ring_at[kind] += 1
            table = d["peer_u_2"] if kind == 0 else d["peer_v_2"]
            G.wait(routed[b][0], ring_free[s])
            g_sem[s][1] += 16
            off = IDX[:, b % 2, n:n + 1]
            nc.gpsimd.indirect_dma_start(
                out=US[:, s, :], out_offset=None, in_=table,
                in_offset=bass.IndirectOffsetOnAxis(ap=off, axis=0)).then_inc(g_sem[s][0], 16)
            return s, (g_sem[s][0], g_sem[s][1])

        units = [(b, h) for b in range(4) for h in range(8)]
        wmark = {}
        dg_ring = Ring(8)
        acc = {}
        routes = {}
        out_marks = []
        ac_free = {}

        def dots(b, h, k):
            n = 16 * h + k
            s, m = gather(0, b, n)
            t = V.op(lambda e, s=s, n=n, b=b: e.tensor_tensor_reduce(
                US[:, s, :], US[:, s, :], HN[:, b, :], 1.0, 0.0, ALU.mult, ALU.add, AC[:, b % 2, n:n + 1]),
                m, xn2, ac_free.get(b - 2))
            ring_free[s] = t
            return t

        def weigh(b, h, t):
            sl = slice(16 * h, 16 * h + 16)
            a = A.op(lambda e: e.activation(AG[:, b % 2, sl], AC[:, b % 2, sl], ACT.Gelu), t, ac_free.get(b - 2))
            wmark[(b, h)] = V.op(lambda e: e.tensor_tensor(AG[:, b % 2, sl], AG[:, b % 2, sl], GW[:, b % 2, sl],
                                                           ALU.mult), a, routed[b][1])

        def rows_sum(b, h, k):
            n = 16 * h + k
            if n == 0:
                acc[b] = pair()
            s, m = gather(1, b, n)
            q, fr = dg_ring.take()
            a = A.op(lambda e, q=q, n=n, b=b: e.activation(DG[:, q, :], I128[:, :], ACT.Copy,
                                                         scale=AG[:, b % 2, n:n + 1]), wmark[(b, h)], fr)
            PE.wait(a, m)
            for half in range(2):
                fn = matmul(PS[:, 2 * acc[b] + half, :], DG[:, q, :], US[:, s, 512 * half:512 * half + 512],
                            n == 0, n == 127)
                t = PE.op(fn) if half else PE.quiet(fn)
            dg_ring.freed[q] = t
            ring_free[s] = t
            return t

        def finish(b, t):
            i = acc[b]
            hb = H[:, b, :]
            v = V.op(lambda e: e.tensor_tensor(hb, hb, flat(i), ALU.add), t, hm[b])
            free(i, v)
            a = squares(hb, 128, b, JP, [v, q_used])
            r = root(1.0 / 1024, EPS, 8, a)
            v = V.op(lambda e: e.scalar_tensor_tensor(out=hb, in0=hb, scalar=RS[:, b:b + 1], in1=GBC[:, :],
                                                      op0=ALU.mult, op1=ALU.mult), r, m_g)
            out_marks.append(once(SP, d["out"][128 * b:128 * b + 128, :], hb, v))

        JP = at("JP2", [128, 1024], F32, pa.off)
        assert pa.off + 4096 <= end
        for n in range(len(units) + 1):
            for k in range(16):
                if n < len(units):
                    b, h = units[n]
                    if h == 0 and k == 0 and b < 3:
                        routes[b + 1] = route(b + 1)
                    if h < 7 and b < 3:
                        next(routes[b + 1], None)
                    t = dots(b, h, k)
                if n > 0:
                    pb_, ph = units[n - 1]
                    tt = rows_sum(pb_, ph, k)
            if n < len(units):
                weigh(b, h, t)
            if n > 0 and ph == 7:
                tile_free[pb_ % 2] = tt
                ac_free[pb_] = tt
                finish(pb_, tt)
        SP.wait(out_marks)



def _tables():
    import numpy as np
    half = 128
    inv = (10000.0 ** (-np.arange(half, dtype=np.float32) / half)).astype(np.float32)
    ang = (np.arange(T, dtype=np.float32)[:, None] * inv[None, :]).astype(np.float32)
    cs = np.stack([np.cos(ang).T, np.sin(ang).T], 1).astype(np.float32)
    lg = np.log(1.0 - 2.0 ** (-5.0 - np.arange(4, dtype=np.float64)))
    m = np.arange(128)[:, None]
    n = np.arange(512)[None, :]
    same = (m // 64 == n // 64) & (n < 128)
    seen = (m // 64 < n // 64) | (n >= 128)
    dist = np.where(same, np.abs(n - m), n - m)
    dec = np.exp(lg[:, None, None] * np.maximum(dist, 0)) * (same | seen) / 16.0
    mm = np.arange(NM)[:, None]
    nn = np.arange(T)[None, :]
    decm = np.exp(lg[:, None, None] * np.abs(nn - mm)) / 16.0
    masks = np.zeros((128, 8, 128), np.float32)
    j = np.arange(128)[:, None]
    i = np.arange(128)[None, :]
    masks[:, 0, :] = i == j
    for lv in range(7):
        s = 1 << lv
        masks[:, lv + 1, :] = (i // (2 * s) == j // (2 * s)) & (i // s % 2 == 1) & (j // s % 2 == 0)
    return {
        "ident": np.eye(128, dtype=np.float32),
        "cos_sin": np.ascontiguousarray(cs),
        "decay": dec.astype(np.float32),
        "decay_meta": decm.astype(np.float32),
        "masks": masks,
        "iota": np.arange(16, dtype=np.float32),
    }


def _layout(w):
    import numpy as np
    out = {}

    def kn(m):
        k = m.shape[0] // 128
        return m.reshape(k, 128, m.shape[1]).transpose(1, 0, 2).reshape(128, -1)

    blocks = []
    for l in range(DEPTH):
        wi = w["w_in"][l]
        for j in range(8):
            a = 128 * j
            blocks.append(kn(np.concatenate([wi[:, a:a + 128], wi[:, 2048 + a:2176 + a]], 1)))
            blocks.append(kn(np.concatenate([wi[:, 1024 + a:1152 + a], wi[:, 3072 + a:3200 + a]], 1)))
        for g in range(4):
            blocks.append(kn(wi[:, 10240 + 256 * g:10496 + 256 * g]))
            blocks.append(kn(w["w_conv_out"][l][:, 256 * g:256 * g + 256]))
        def ret(h):
            m = w["w_ret_out"][l][512 * h:512 * h + 512]
            return [kn(m[:, 0:512]), kn(m[:, 512:1024])]
        for h in range(4):
            blocks.append(kn(wi[:, 4096 + 256 * h:4352 + 256 * h]))
            blocks.append(kn(wi[:, 5120 + 256 * h:5376 + 256 * h]))
            blocks.append(kn(wi[:, 6144 + 512 * h:6400 + 512 * h]))
            blocks.append(kn(wi[:, 6400 + 512 * h:6656 + 512 * h]))
            if h > 0:
                blocks += ret(h - 1)
            blocks.append(kn(wi[:, 8192 + 512 * h:8448 + 512 * h]))
            blocks.append(kn(wi[:, 8448 + 512 * h:8704 + 512 * h]))
        blocks += ret(3)
        for g in range(4):
            blocks.append(kn(wi[:, 11264 + 256 * g:11520 + 256 * g]))
        for g in range(4):
            blocks.append(kn(w["w_o"][l][:, 256 * g:256 * g + 256]))
    w2 = w["w_in_2"][0]
    starts = [0, 256, 512, 768, 2048, 2304, 1024, 1280, 2560, 2816, 1536, 1792, 3088, 3344]
    for a in starts:
        blocks.append(kn(w2[:, a:a + 256]))
    for g in range(4):
        blocks.append(kn(w["w_out_2"][0][:, 256 * g:256 * g + 256]))
    for g in range(8):
        blocks.append(kn(w["peer_w_q_2"][0][:, 256 * g:256 * g + 256]))
    out["blocks"] = np.stack(blocks)
    assert len(blocks) == DEPTH * BLOCKS_LAYER + BLOCKS_SECOND

    def tiles(v):
        return np.ascontiguousarray(v.reshape(-1, 128).T)

    out["x"] = np.ascontiguousarray(w["x"][0])
    out["meta"] = w["meta"]
    out["pre_norm_g"] = w["pre_norm_g"]
    out["post_norm_g"] = w["post_norm_g"]
    out["b_in"] = w["b_in"]
    out["b_in_T"] = np.stack([tiles(w["b_in"][l]) for l in range(DEPTH)])
    out["conv_w_T"] = np.stack([tiles(w["conv_w"][l]) for l in range(DEPTH)])
    out["conv_b_T"] = np.stack([tiles(w["conv_b"][l]) for l in range(DEPTH)])
    out["gn_g_T"] = np.stack([tiles(w["ret_gn_g"][l]) for l in range(DEPTH)])
    out["norm1_g_2"] = w["norm1_g_2"]
    out["norm2_g_2"] = w["norm2_g_2"]
    out["norm_f_g_2"] = w["norm_f_g_2"]
    out["logits_T"] = tiles(w["hg_lower_logits_2"])
    out["small_T"] = np.ascontiguousarray(np.concatenate(
        [tiles(w["hg_norm_g_2"]), tiles(w["gla_norm_g_2"]), tiles(w["gla_b_gate_2"])], 1))
    out["w_glow"] = np.ascontiguousarray(w2[:, 3072:3088].reshape(8, 128, 16).transpose(1, 0, 2))
    out["gla_w_gate_up_2"] = w["gla_w_gate_up_2"]
    out["keys_T"] = np.ascontiguousarray(w["peer_sub_keys_2"][0].reshape(16, 128, 128).transpose(2, 0, 1))
    out["peer_u_2"] = w["peer_u_2"][0]
    out["peer_v_2"] = w["peer_v_2"][0]
    return out


def kernel(**inputs):
    import numpy as np
    import concourse.bacc as bacc
    from concourse.bass_utils import run_bass_kernel_spmd

    arrays = dict(_layout({k: np.asarray(v) for k, v in inputs.items()}))
    arrays.update(_tables())
    nc = bacc.Bacc("TRN2", target_bir_lowering=False, num_devices=1)
    feeds, d = {}, {}
    for name, a in arrays.items():
        a = np.ascontiguousarray(a)
        feeds["in_" + name] = a
        d[name] = nc.dram_tensor("in_" + name, a.shape, mybir.dt.from_np(a.dtype), kind="ExternalInput").ap()
    d["hx"] = nc.dram_tensor("rows", (512, 1024), F32, kind="Internal").ap()
    d["out"] = nc.dram_tensor("out_0", (512, 1024), F32, kind="ExternalOutput").ap()
    two_blocks(nc, d)
    r = run_bass_kernel_spmd(nc, [feeds], core_ids=[0])
    return np.asarray(r.results[0]["out_0"]).reshape(1, 512, 1024)
```

```python
from contextlib import ExitStack

import concourse.bass as bass
from concourse import mybir

F32 = mybir.dt.float32
R32 = mybir.dt.float32r
U32 = mybir.dt.uint32
U8 = mybir.dt.uint8
ALU = mybir.AluOpType
ACT = mybir.ActivationFunctionType
AX = mybir.AxisListType

T = 528
NM = 16
WA = 272
KB = 1024
NRAW = 6
NSPLIT = 4
DEPTH = 2
EPS = 1e-6
GN_EPS = 1e-5
LOWEST = -3.0e38
BLOCKS_LAYER = 64
BLOCKS_SECOND = 26
NSLOT = 4
NDG = 4
EARLY = 244
ON_PE = 3
LATE = 2
P_CONV = 1.0
P_GA = 1.0
P_HEAD = 1.15
P_GB = 0.2
P_WO = 1.8
P_SECOND = 0.8
P_QP = 1.6
ROUTE_COST = 0.8
PAIR_COST = 1.5


class Queue:

    def __init__(self, engine, sem, serial=False):
        self.engine, self.sem, self.n, self.seen, self.serial = engine, sem, 0, {}, serial

    def wait(self, *marks):
        for m in marks:
            if m is None:
                continue
            if isinstance(m, list):
                self.wait(*m)
                continue
            sem, value = m
            if self.seen.get(id(sem), 0) < value:
                self.seen[id(sem)] = value
                self.engine.wait_ge(sem, value)

    def op(self, fn, *marks, loose=False):
        self.wait(*marks)
        if self.serial and self.n and not loose:
            self.wait((self.sem, self.n))
        self.n += 1
        fn(self.engine).then_inc(self.sem, 1)
        return (self.sem, self.n)

    def quiet(self, fn, *marks):
        self.wait(*marks)
        fn(self.engine)

    def dma(self, slot, out, in_, *marks):
        self.wait(*marks)
        slot[1] += 16
        self.engine.dma_start(out, in_).then_inc(slot[0], 16)
        return (slot[0], slot[1])


class Ring:

    def __init__(self, n):
        self.n, self.at, self.freed = n, 0, [None] * n

    def take(self):
        i = self.at % self.n
        self.at += 1
        return i, self.freed[i]


def two_blocks(nc, d):
    ctx = ExitStack()
    with ctx:
        sems = []

        def sem(name):
            s = ctx.enter_context(nc.semaphore(name))
            sems.append(s)
            return s

        def slot(name):
            return [sem(name), 0]

        PE = Queue(nc.tensor, sem("q_pe"))
        V = Queue(nc.vector, sem("q_dve"), True)
        A = Queue(nc.scalar, sem("q_act"), True)
        G = Queue(nc.gpsimd, sem("q_pool"))
        SP = Queue(nc.sync, sem("q_sp"))

        base = nc.sbuf_base
        base += (-base) % 64
        top = [base]

        def at(name, shape, dt, off):
            return nc.alloc_sbuf_tensor_at(name, shape, dt, offset=off)

        def put(name, shape, dt=F32):
            size = 4 if dt != U8 else 1
            for s in shape[1:]:
                size *= s
            off = top[0]
            top[0] += size + (-size) % 32
            return at(name, shape, dt, off)

        def area(size):
            off = top[0]
            top[0] += size + (-size) % 32
            return off

        RAW = put("RAW", [128, NRAW, KB])
        WH = put("WH", [128, NSPLIT, KB], R32)
        WL = put("WL", [128, NSPLIT, KB], R32)
        x_area = area(0)
        XH = put("XH", [128, 8, WA], R32)
        XL = put("XL", [128, 8, WA], R32)
        I128 = put("I128", [128, 128])
        BIN = put("BIN", [128, 96])
        CW = put("CW", [128, 24])
        CB = put("CB", [128, 8])
        GNG = put("GNG", [128, 16])
        UL = put("UL", [128, DEPTH, 8, 2])
        LGT = put("LGT", [128, 8])
        LBS = put("LBS", [128, 6, 4])
        VG = put("VG", [128, 4])
        SS = put("SS", [128, 8])
        RS = put("RS", [128, 8])
        GBC = put("GBC", [128, 1024])
        GF = put("GF", [128, 1024])
        IO = put("IO", [128, 16])
        SW = put("SW", [128, 8, 4])
        SF = put("SF", [128, 2])
        SSP = put("SSP", [128, 3, 4])
        RP3 = put("RP3", [128, 3])
        HA = put("HA", [128, 2, 1024])
        HNA = put("HNA", [128, 2, 1024])
        US = put("US", [128, 2 * NSLOT, 1024])
        DG = put("DG", [128, NDG, 128])
        IDX = put("IDX", [128, 4, 128], U32)
        GW = put("GW", [128, 4, 128])
        AC = put("AC", [128, 4, 128])
        AG = AC
        HM = put("HM", [16, 1024])
        HW = put("HW", [128, 2, 1024])
        h_area = top[0] - 12288
        r_area = top[0]
        end = nc.sbuf_usable_end

        class Area:
            def __init__(self, off):
                self.off = off

            def put(self, name, shape, dt=F32):
                size = 4
                for s in shape[1:]:
                    size *= s
                o = self.off
                self.off += size + (-size) % 32
                assert self.off <= end, (name, self.off, end)
                return at(name, shape, dt, o)

        PS = ctx.enter_context(nc.psum_tensor("PS", [128, 8, 512], F32))
        singles, pairs = Ring(4), Ring(1)

        def bank():
            i, mark = singles.take()
            PE.wait(mark)
            return i

        def free(i, mark):
            singles.freed[i] = mark

        def pair():
            i, mark = pairs.take()
            PE.wait(mark)
            return PS[:, 4:6, :].rearrange("p a b -> p (a b)")

        def free_pair(mark):
            pairs.freed[0] = mark

        ACC = PS[:, 6:8, :].rearrange("p a b -> p (a b)")

        def f32(x):
            return x.bitcast(F32)

        def now():
            return [(q.sem, q.n) for q in (PE, V, A) if q.n]

        raw_sem = [slot(f"raw{i}") for i in range(NRAW)]
        n_halves = 2 * (DEPTH * BLOCKS_LAYER + BLOCKS_SECOND)
        total = 2 * n_halves
        landed, high_done, split_done, used = {}, {}, {}, {}
        state = {"load": 0, "high": 0, "low": 0, "use": 0}

        def load_half(after=None):
            j = state["load"]
            if j < total:
                landed[j] = SP.dma(raw_sem[j % NRAW], RAW[:, j % NRAW, :], d["halves"][j % n_halves], after)
                state["load"] += 1

        def high_half():
            j = state["high"]
            hi, raw = WH[:, j % NSPLIT, :], RAW[:, j % NRAW, :]
            high_done[j] = A.op(lambda e: e.activation(hi, raw, ACT.Copy), landed[j], used.get(j - NSPLIT), loose=True)
            state["high"] += 1

        def low_half():
            j = state["low"]
            hi, lo, raw = WH[:, j % NSPLIT, :], WL[:, j % NSPLIT, :], RAW[:, j % NRAW, :]
            t = V.op(lambda e: e.tensor_tensor(lo, raw, f32(hi), ALU.subtract), high_done[j], loose=True)
            split_done[j] = t
            state["low"] += 1
            load_half(t)

        def split_ahead(needed):
            while state["low"] < state["high"]:
                low_half()
            while state["high"] < total and (state["high"] < NSPLIT or state["high"] - NSPLIT in used):
                high_half()
            while state["low"] <= needed:
                low_half()

        def block(nk):
            j = state["use"]
            state["use"] += 1
            split_ahead(2 * j)
            s0 = 2 * j % NSPLIT
            hi = WH[:, s0:s0 + 2, :].rearrange("p h (k n) -> p h k n", k=nk)
            lo = WL[:, s0:s0 + 2, :].rearrange("p h (k n) -> p h k n", k=nk)
            return j, hi, lo

        def done_with(blk, mark):
            for half in range(2):
                used.setdefault(2 * blk[0] + half, mark)

        background = []
        credit = [0.0]

        pace = [1.0]

        def pump(worth=1.0):
            credit[0] += worth * pace[0]
            while credit[0] > 0 and background:
                cost = next(background[0], None)
                if cost is None:
                    background.pop(0)
                else:
                    credit[0] -= cost
            if not background:
                credit[0] = 0

        def matmul(out, lhsT, rhs, first, last):
            return lambda e: e.matmul(out, lhsT, rhs, start=first, stop=last)

        def product_T(blk, c, nk, mh, ml, lo, hi_col, ready):
            j, wh, wl = blk
            half, c = (c, 0) if nk == 8 else (c // 2, c % 2)
            split_ahead(2 * j + half)
            i = bank()
            PE.wait(ready, split_done[2 * j + half])
            out = PS[:, i, 0:hi_col - lo]
            for k in range(nk):
                for n, (s, m) in enumerate(((wh, mh), (wh, ml), (wl, mh))):
                    fn = matmul(out, s[:, half, k, 128 * c:128 * c + 128], m[:, k, lo:hi_col],
                                k == 0 and n == 0, k == nk - 1 and n == 2)
                    mark = PE.op(fn) if k == nk - 1 and n == 2 else PE.quiet(fn)
            if nk == 8 or c == 1:
                used[2 * j + half] = mark
            pump(nk / 8)
            return i, out, mark

        def product_rows(blk, xh, xl, starts, ready):
            j, wh, wl = blk
            split_ahead(2 * j + 1)
            i = bank()
            PE.wait(ready, split_done[2 * j], split_done[2 * j + 1])
            for q, a in enumerate(starts):
                for k in range(8):
                    for n, (s, m) in enumerate(((xh, wh), (xh, wl), (xl, wh))):
                        fn = matmul(PS[:, i, 256 * q:256 * q + 256], s[:, k, a:a + 128], m[:, :, k, :],
                                    k == 0 and n == 0, k == 7 and n == 2)
                        mark = PE.op(fn) if k == 7 and n == 2 and q == len(starts) - 1 else PE.quiet(fn)
                pump()
            return i, PS[:, i, :].rearrange("p (b n) -> p b n", b=2), mark

        def split_to(hi, lo, src, ready, free_of=None):
            t = A.op(lambda e: e.activation(hi, src, ACT.Copy), ready, free_of)
            return V.op(lambda e: e.tensor_tensor(lo, src, f32(hi), ALU.subtract), t)

        misc = [0]

        def once(q, out, in_, *marks):
            misc[0] += 1
            return q.dma(slot(f"m{misc[0]}"), out, in_, *marks)

        reused = {}

        def again(name, q, out, in_, *marks):
            if name not in reused:
                reused[name] = slot(name)
            return q.dma(reused[name], out, in_, *marks)

        def root(mean_scale, eps, n, ready):
            t = V.op(lambda e: e.tensor_scalar(SS[:, 0:n], SS[:, 0:n], mean_scale, eps, ALU.mult, ALU.add), ready)
            t = A.op(lambda e: e.activation(RS[:, 0:n], SS[:, 0:n], ACT.Sqrt), t)
            return V.op(lambda e: e.reciprocal(RS[:, 0:n], RS[:, 0:n]), t)

        m_id = once(SP, I128[:, :], d["ident"])
        m_ss = V.op(lambda e: e.memset(SS[:, :], 1.0))
        m_rs = V.op(lambda e: e.memset(RS[:, :], 1.0))
        m_ssp = V.op(lambda e: e.memset(SSP[:, :, :], 1.0))
        m_gf = once(SP, GF[:, :], d["norm_f_g_2"].partition_broadcast(128))
        m_io = once(SP, IO[:, :], d["iota"].partition_broadcast(128))
        m_lgt = once(SP, LGT[:, :], d["logits_T"])
        m_vg = once(SP, VG[:, :], d["small_T"])

        l0, l1 = LGT[:, 0:4], LGT[:, 4:8]
        B = [LBS[:, n, :] for n in range(6)]
        t = V.op(lambda e: e.tensor_tensor(B[0], l0, l1, ALU.max), m_lgt)
        t = V.op(lambda e: e.tensor_tensor(B[1], l0, B[0], ALU.subtract), t)
        t1 = V.op(lambda e: e.tensor_tensor(B[2], l1, B[0], ALU.subtract), t)
        t = A.op(lambda e: e.activation(B[3], B[1], ACT.Exp), t, t1)
        t = A.op(lambda e: e.activation(B[4], B[2], ACT.Exp), t)
        t = V.op(lambda e: e.tensor_tensor(B[5], B[3], B[4], ALU.add), t)
        t = V.op(lambda e: e.reciprocal(B[0], B[5]), t)
        t = V.op(lambda e: e.tensor_tensor(B[1], B[3], B[0], ALU.mult), t)
        m_lb = V.op(lambda e: e.tensor_scalar(B[2], B[1], -1.0, 1.0, ALU.mult, ALU.add), t)
        LB, LB1 = B[1], B[2]

        def squares(src, rows, n, junk, ready):
            return A.op(lambda e: e.activation(junk[0:rows, :], src, ACT.Square,
                                               accum_out=SS[0:rows, n:n + 1]), ready)

        def transposed(tiles, gains, gain, ready, xt, junk, keep=None, x_free=None):
            free_xt = [None, None]
            rows_in, out_of = {}, {}

            def come(k):
                n = tiles[k][3]
                rows_in[k] = ready[n]() if callable(ready[n]) else ready[n]

            def scale(k):
                rows, src, col, n = tiles[k]
                ss, rs = SS[0:rows, n:n + 1], RS[0:rows, n:n + 1]
                t = A.op(lambda e: e.activation(junk[0:rows, :], src, ACT.Square, accum_out=ss),
                         [rows_in[k], m_ss, x_free])
                t = V.op(lambda e: e.tensor_scalar(ss, ss, 1.0 / 1024, EPS, ALU.mult, ALU.add), t, m_rs, loose=True)
                t = A.op(lambda e: e.activation(rs, ss, ACT.Sqrt), t)
                t = V.op(lambda e: e.reciprocal(rs, rs), t)
                buf = xt[0:rows, k % 2, :] if keep is None else keep[:, n, :]
                t = V.op(lambda e: e.scalar_tensor_tensor(
                    out=buf, in0=src, scalar=rs, in1=gains[0:rows, :], op0=ALU.mult, op1=ALU.mult),
                    t, gain, free_xt[k % 2], x_free)
                out_of[k] = []
                for half in range(2):
                    i = bank()
                    PE.wait(t, m_id)
                    v = PS[:, i, :].rearrange("p (k n) -> p k n", k=4)
                    for kc in range(4):
                        c = 512 * half + 128 * kc
                        fn = lambda e: e.transpose(v[:, kc, 0:rows], buf[:, c:c + 128], I128[0:rows, 0:rows])
                        tt = PE.op(fn) if kc == 3 else PE.quiet(fn)
                    out_of[k].append((i, v, tt))
                free_xt[k % 2] = tt

            def leave(k):
                rows, src, col, n = tiles[k]
                for half, (i, v, tt) in enumerate(out_of[k]):
                    sl = slice(4 * half, 4 * half + 4)
                    t = split_to(XH[:, sl, col:col + rows], XL[:, sl, col:col + rows], v[:, :, 0:rows], tt, x_free)
                    free(i, t)
                return t

            come(0)
            come(1)
            scale(0)
            done = []
            if len(tiles) == 3:
                come(2)
            scale(1)
            done.append(leave(0))
            if len(tiles) == 3:
                scale(2)
            done += [leave(k) for k in range(1, len(tiles))]
            return done

        r0 = Area(r_area)
        YA = r0.put("YA", [128, 8, WA])
        YB = r0.put("YB", [128, 8, WA])
        c0 = r0.off
        cv = Area(r_area)
        CH = Area(c0).put("CH", [128, 8, WA], R32)
        CL = Area(c0 + 8704).put("CL", [128, 8, WA], R32)
        cv = Area(c0 + 17408)
        UB = cv.put("UB", [128, 2, WA + 2])
        HS = cv.put("HS", [128, WA])
        ZS = cv.put("ZS", [128, 2, WA])
        YC = cv.put("YC", [128, 2, WA])
        conv_top = cv.off
        xa = Area(c0)
        XT = xa.put("XT", [128, 2, 1024])
        JK = xa.put("JK", [128, 1024])
        hd = Area(c0)
        QK = hd.put("QK", [128, 4, WA])
        KP = hd.put("KP", [128, 2, WA])
        SX = hd.put("SX", [128, 896])
        SM = hd.put("SM", [16, WA])
        OO = Area(hd.off).put("OO", [128, 3, 512])
        RP = hd.put("RP", [128, 3, 2, WA])
        CS = hd.put("CS", [128, 2, WA])
        RH = hd.put("RH", [128, 4, WA], R32)
        RL = hd.put("RL", [128, 4, WA], R32)
        Z = hd.put("Z", [128, 4, WA])
        DT = hd.put("DT", [128, 512])
        DMT = hd.put("DMT", [16, WA])
        BV = hd.put("BV", [128, 512])
        ST = hd.put("ST", [128, 3, 6])
        MV = hd.put("MV", [128, 3, 2])
        hp = Area(h_area)
        VV = hp.put("VV", [128, 3, 512])
        VP = hp.put("VP", [128, 3, 512])
        assert hp.off <= r_area
        fy = Area(c0)
        YH = fy.put("YH", [128, 8, WA], R32)
        YL = fy.put("YL", [128, 8, WA], R32)
        TG = fy.put("TG", [128, 2, WA])
        GB2 = fy.put("GB2", [128, 1024])
        Y2a = Area(r_area)
        Y2 = Y2a.put("Y2", [128, 2, 1024])
        Y2M = Y2a.put("Y2M", [16, 1024])
        JY = Y2a.put("JY", [128, 1024])
        assert Y2a.off <= c0
        ha = Area(h_area)
        V2 = ha.put("V2", [128, 2, 1024])
        WGL = ha.put("WGL", [128, 8, 16])
        GLT = ha.put("GLT", [16, 256])
        UPW = ha.put("UPW", [16, 256])
        assert ha.off <= r_area
        sa = Area(r_area)
        Q6 = sa.put("Q6", [128, 6, 256])
        K6 = sa.put("K6", [128, 6, 256])
        F6 = sa.put("F6", [128, 6, 256])
        G6 = sa.put("G6", [128, 6, 256])
        GT = sa.put("GT", [128, 8, 256])
        SD = sa.put("SD", [128, 8, 256])
        MK = sa.put("MK", [128, 8, 128])
        S1 = sa.put("S1", [128, 8, 128])
        V2P = sa.put("V2P", [128, 2, 1024])
        S2 = Area(x_area).put("S2", [128, 8, 2, 256])
        ma = Area(r_area)
        MH = ma.put("MH", [128, 8, 256], R32)
        ML = ma.put("ML", [128, 8, 256], R32)
        OT = ma.put("OT", [128, 1024])
        SQ = ma.put("SQ", [128, 1024])
        assert ma.off <= r_area + 4 * 6144
        pa = Area(r_area)
        KT = pa.put("KT", [128, 16, 128])
        pa.off = conv_top
        SC = pa.put("SC", [128, 16, 128])
        TV = pa.put("TV", [128, 16, 16])
        TI = pa.put("TI", [128, 16, 16], U32)
        TF = pa.put("TF", [128, 16, 16])
        BV8 = pa.put("BV8", [128, 8, 16])
        BP = pa.put("BP", [128, 8, 16], U32)
        BI = pa.put("BI", [128, 2, 128], U32)
        BF = pa.put("BF", [128, 2, 128])
        EF = pa.put("EF", [128, 2, 128])
        route_top = pa.off
        pb = Area(h_area)
        second_of = [pb.put("TV1", [128, 16, 16]), pb.put("TI1", [128, 16, 16], U32), pb.put("TF1", [128, 16, 16]),
                     pb.put("BV81", [128, 8, 16]), pb.put("BP1", [128, 8, 16], U32)]
        SC2 = Area(r_area + 8704).put("SC2", [128, 16, 128])
        QP = Area(c0).put("QP", [128, 16, 256])
        HNB = Area(c0 + 16384).put("HNB", [128, 2, 1024])
        assert c0 + 16384 + 8192 <= conv_top

        passed, fetched = [], []
        routed = {}
        hm_all = {}
        hn_ready = {}
        gather_start = []
        res = {0: HA, 1: HW}
        hn_of = {0: HNA, 1: HNB}

        def top16(groups, ready):
            m = [ready] * len(groups)

            def each(fn):
                for n, g in enumerate(groups):
                    m[n] = V.op(lambda e: fn(e, *g), m[n], loose=True)

            each(lambda e, src, vals, idx: e.max(vals[:, 0:8], src))
            each(lambda e, src, vals, idx: e.max_index(idx[:, 0:8], vals[:, 0:8], src))
            each(lambda e, src, vals, idx: e.match_replace(src, vals[:, 0:8], src, LOWEST))
            each(lambda e, src, vals, idx: e.max(vals[:, 8:16], src))
            each(lambda e, src, vals, idx: e.max_index(idx[:, 8:16], vals[:, 8:16], src))
            return list(m)

        top_of = [(SC, TV, TI, TF, BV8, BP), (SC2, *second_of)]

        def sub_scores(g, qpm, m_kt, free_of):
            i = bank()
            PE.wait(qpm, m_kt)
            for b in range(2):
                for c in range(2):
                    t = PE.op(matmul(PS[:, i, 256 * b + 128 * c:256 * b + 128 * c + 128],
                                     QP[:, 2 * g + c, 128 * b:128 * b + 128], KT[:, 2 * g + c, :], True, True))
            out = []
            for b in range(2):
                dest = top_of[b][0][:, 2 * g:2 * g + 2, :].rearrange("p a b -> p (a b)")
                out.append(A.op(lambda e: e.activation(dest, PS[:, i, 256 * b:256 * b + 256], ACT.Copy), t, free_of))
            free(i, out[-1])
            return out

        def top_keys(b, g, sc, prior):
            src, vals, idx = top_of[b][0:3]
            return top16([(src[:, n, :], vals[:, n, :], idx[:, n, :]) for n in (2 * g, 2 * g + 1)], [sc, prior])

        def route(gb, t, late):
            src, TV, TI, TF, BV8, BP = top_of[gb % 2]
            for g, sc, prior in late:
                t = top_keys(gb % 2, g, sc, prior)
                yield ROUTE_COST
            tf = V.op(lambda e: e.tensor_copy(TF[:, :, :], TI[:, :, :]), t)
            cand = src[:, :, :].rearrange("p (h two) n -> p h (two n)", two=2)
            tv = TV[:, :, :].rearrange("p (h two) n -> p h two n", two=2)
            tfv = TF[:, :, :].rearrange("p (h two) n -> p h two n", two=2)
            t = V.op(lambda e: e.tensor_tensor(
                cand.rearrange("p h (i j) -> p h i j", i=16),
                tv[:, :, 0, :].unsqueeze(3).broadcast_to([128, 8, 16, 16]),
                tv[:, :, 1, :].unsqueeze(2).broadcast_to([128, 8, 16, 16]), ALU.add), t)
            yield ROUTE_COST
            first = [t]
            for h in range(0, 8, 2):
                t = top16([(cand[:, h + q, :], BV8[:, h + q, :], BP[:, h + q, :]) for q in range(2)], first)
                yield 2 * ROUTE_COST
            bp = BP[:, :, :].rearrange("p h k -> p (h k)")
            t = V.op(lambda e: e.tensor_scalar(BI[:, 0, :], bp, 4, None, ALU.logical_shift_right), t)
            t = V.op(lambda e: e.tensor_scalar(BI[:, 1, :], bp, 15, None, ALU.bitwise_and), t)
            t = V.op(lambda e: e.tensor_copy(BF[:, :, :], BI[:, :, :]), t)
            eq_area = src[:, :, :].rearrange("p a b -> p (a b)")
            eq = eq_area.rearrange("p (h k a) -> p h k a", h=8, k=16)
            flat_eq = eq_area.rearrange("p (hk a) -> p hk a", a=16)
            for n in range(2):
                t = V.op(lambda e: e.tensor_tensor(
                    flat_eq, BF[:, n, :].unsqueeze(2).broadcast_to([128, 128, 16]),
                    IO[:, :].unsqueeze(1).broadcast_to([128, 128, 16]), ALU.is_equal), t, m_io)
                yield ROUTE_COST
                t = V.op(lambda e: e.tensor_tensor(
                    eq, eq, tfv[:, :, n, :].unsqueeze(2).broadcast_to([128, 8, 16, 16]), ALU.mult), t, tf)
                t = V.op(lambda e: e.tensor_reduce(EF[:, n, :], flat_eq, AX.X, ALU.add), t)
                yield ROUTE_COST
            t = V.op(lambda e: e.scalar_tensor_tensor(out=EF[:, 0, :], in0=EF[:, 0, :], scalar=128.0,
                                                      in1=EF[:, 1, :], op0=ALU.mult, op1=ALU.add), t)
            idx = V.op(lambda e: e.tensor_copy(IDX[:, gb, :], EF[:, 0, :]), t)
            gw = GW[:, gb, :].rearrange("p (h k) -> p h k", h=8)
            t = V.op(lambda e: e.tensor_tensor(gw, BV8[:, :, :], BV8[:, :, 0:1].broadcast_to([128, 8, 16]),
                                               ALU.subtract), idx)
            t = A.op(lambda e: e.activation(GW[:, gb, :], GW[:, gb, :], ACT.Exp), t)
            t = V.op(lambda e: e.tensor_reduce(SW[:, :, 0], gw, AX.X, ALU.add), t)
            t = V.op(lambda e: e.reciprocal(SW[:, :, 1], SW[:, :, 0]), t)
            t = V.op(lambda e: e.tensor_tensor(gw, gw, SW[:, :, 1:2].broadcast_to([128, 8, 16]), ALU.mult), t)
            routed[gb] = (idx, t)
            yield ROUTE_COST

        g_sem = [slot(f"g{n}") for n in range(2 * NSLOT)]
        ring_free = [None] * (2 * NSLOT)
        ring_at = [0, 0]
        wmark = {}
        dg_ring = Ring(NDG)
        acc_free = [None]
        out_marks = []
        added, summed = {}, {}
        shared = [True]

        def gather(kind, gb, n):
            s = NSLOT * kind + ring_at[kind] % NSLOT
            ring_at[kind] += 1
            G.wait(routed[gb][0], ring_free[s])
            g_sem[s][1] += 16
            nc.gpsimd.indirect_dma_start(
                out=US[:, s, :], out_offset=None, in_=d["peer_u_2"] if kind == 0 else d["peer_v_2"],
                in_offset=bass.IndirectOffsetOnAxis(ap=IDX[:, gb, n:n + 1], axis=0)).then_inc(g_sem[s][0], 16)
            return s, (g_sem[s][0], g_sem[s][1])

        def dots(gb, h, k):
            n = 16 * h + k
            s, m = gather(0, gb, n)
            t = V.op(lambda e: e.tensor_tensor_reduce(
                US[:, s, :], US[:, s, :], hn_of[gb // 2][:, gb % 2, :], 1.0, 0.0, ALU.mult, ALU.add,
                AC[:, gb, n:n + 1]), m, hn_ready[gb // 2], loose=True)
            ring_free[s] = t
            return t

        def weigh(gb, h, t):
            sl = slice(16 * h, 16 * h + 16)
            a = A.op(lambda e: e.activation(AG[:, gb, sl], AC[:, gb, sl], ACT.Gelu), t)
            wmark[(gb, h)] = V.op(lambda e: e.tensor_tensor(AG[:, gb, sl], AG[:, gb, sl], GW[:, gb, sl], ALU.mult),
                                  a, routed[gb][1])

        def rows_sum(gb, h, k):
            n = 16 * h + k
            if n == 0:
                PE.wait(acc_free[0])
            s, m = gather(1, gb, n)
            if shared[0] and n % ON_PE and n < 127:
                hb = HA[:, gb, :]
                t = V.op(lambda e: e.scalar_tensor_tensor(
                    out=hb, in0=US[:, s, :], scalar=AG[:, gb, n:n + 1], in1=hb, op0=ALU.mult, op1=ALU.add),
                    m, hm_all[0], wmark[(gb, h)], added.get(gb), loose=True)
                added[gb] = ring_free[s] = t
                return t
            q, fr = dg_ring.take()
            a = A.op(lambda e: e.activation(DG[:, q, :], I128[:, :], ACT.Copy, scale=AG[:, gb, n:n + 1]),
                     wmark[(gb, h)], fr, m_id, loose=True)
            PE.wait(a, m)
            for half in range(2):
                fn = matmul(ACC[:, 512 * half:512 * half + 512], DG[:, q, :], US[:, s, 512 * half:512 * half + 512],
                            n == 0, n == 127)
                t = PE.op(fn) if half else PE.quiet(fn)
            dg_ring.freed[q] = t
            ring_free[s] = summed[gb] = t
            return t

        def finish(gb, t):
            hb = res[gb // 2][:, gb % 2, :]
            junk = hn_of[gb // 2][:, gb % 2, :]
            v = V.op(lambda e: e.tensor_tensor(hb, hb, ACC, ALU.add), t, summed[gb], hm_all[gb // 2])
            acc_free[0] = v
            a = A.op(lambda e: e.activation(junk, hb, ACT.Square, accum_out=SF[:, 0:1]), v)
            v = V.op(lambda e: e.tensor_scalar(SF[:, 0:1], SF[:, 0:1], 1.0 / 1024, EPS, ALU.mult, ALU.add), a)
            a = A.op(lambda e: e.activation(SF[:, 1:2], SF[:, 0:1], ACT.Sqrt), v)
            v = V.op(lambda e: e.reciprocal(SF[:, 1:2], SF[:, 1:2]), a)
            v = V.op(lambda e: e.scalar_tensor_tensor(out=hb, in0=hb, scalar=SF[:, 1:2], in1=GF[:, :],
                                                      op0=ALU.mult, op1=ALU.mult), v, m_gf)
            out_marks.append(once(SP, d["out"][128 * gb:128 * gb + 128, :], hb, v))

        def gathers(tiles):
            units = [(gb, h) for gb in tiles for h in range(8)]
            for n in range(len(units) + 1):
                for k in range(16):
                    if n < len(units):
                        gb, h = units[n]
                        t = dots(gb, h, k)
                    if n > 0:
                        pb, ph = units[n - 1]
                        tt = rows_sum(pb, ph, k)
                    yield PAIR_COST
                if n < len(units):
                    weigh(gb, h, t)
                if n > 0 and ph == 7:
                    finish(pb, tt)

        def rows_in(grp, *marks):
            ready = {}
            for b in range(2):
                row = 256 * grp + 128 * b
                ready[b] = again(f"hb{b}", SP, HW[:, b, :], d["x"][row:row + 128, :], *marks)
            if grp == 0:
                ready[2] = again("hb2", SP, HM[:, :], d["meta"])
            return ready

        def layers(grp):
            W = WA if grp == 0 else 256
            xo = NM if grp == 0 else 0
            ready = rows_in(grp) if grp == 0 else fetched[0]
            all_tiles = [(128, HW[:, b, :], xo + 128 * b, b) for b in range(2)]
            x_tiles = list(all_tiles)
            if grp == 0:
                all_tiles.append((NM, HM[:, :], 0, 2))
            region_free, gbc_free, par_free, parked = list(passed), list(passed), list(passed), None
            m_in = again("gb2", SP, GB2[:, :], d["pre_norm_g"][0].partition_broadcast(128),
                         hn_ready[0] if grp else None)

            for l in range(DEPTH):
                lo = NM if grp == 0 and l + 1 == DEPTH else 0
                meta_rows = grp == 0 and lo == 0
                if grp == 0 and l == 0:
                    for _ in range(NRAW):
                        load_half()
                m_bin = again("bin", SP, BIN[:, :], d["b_in_T"][l], par_free)
                m_cw = again("cw", SP, CW[:, :], d["conv_w_T"][l], par_free)
                m_cb = again("cb", SP, CB[:, :], d["conv_b_T"][l], par_free)
                m_gn = again("gng", SP, GNG[:, :], d["gn_g_T"][l], par_free)
                xn = transposed(all_tiles, GB2, m_in, ready, XT, JK, x_free=region_free)

                pace[0] = P_CONV
                conv_done = []
                yc_free = [None, None]
                for j in range(8):
                    q = j % 2
                    b1 = block(8)
                    i1, p_h, t_h = product_T(b1, 0, 8, XH, XL, 0, W, xn)
                    a1 = A.op(lambda e: e.activation(HS[:, 0:W], p_h, ACT.Identity, bias=BIN[:, j:j + 1]),
                              t_h, m_bin, conv_done[-1:] or xn)
                    free(i1, a1)
                    i2, p_c, t_c = product_T(b1, 1, 8, XH, XL, 0, W, None)
                    done_with(b1, t_c)
                    if grp == 0:
                        z0 = V.op(lambda e: e.memset(UB[:, q, 0:2], 0.0), yc_free[q] or xn)
                    else:
                        z0 = V.op(lambda e: e.tensor_copy(UB[:, q, 0:2], UL[:, l, j, :]), yc_free[q] or xn)
                    u = V.op(lambda e: e.scalar_tensor_tensor(
                        out=UB[:, q, 2:W + 2], in0=p_c, scalar=BIN[:, 16 + j:17 + j], in1=HS[:, 0:W],
                        op0=ALU.add, op1=ALU.mult), t_c, a1)
                    free(i2, u)
                    if grp == 0:
                        V.op(lambda e: e.tensor_copy(UL[:, l, j, :], UB[:, q, W:W + 2]), u)
                    y = YC[:, q, lo:W]
                    t = A.op(lambda e: e.activation(y, UB[:, q, lo:W], ACT.Identity, bias=CB[:, j:j + 1],
                                                    scale=CW[:, j:j + 1]), u, z0, m_cw, m_cb, yc_free[q])
                    for w in (1, 2):
                        t = V.op(lambda e: e.scalar_tensor_tensor(
                            out=y, in0=UB[:, q, lo + w:W + w], scalar=CW[:, 8 * w + j:8 * w + j + 1], in1=y,
                            op0=ALU.mult, op1=ALU.add), t)
                    b2 = block(8)
                    i3, p_b, t_b = product_T(b2, 0, 8, XH, XL, lo, W, None)
                    t = V.op(lambda e: e.scalar_tensor_tensor(
                        out=y, in0=p_b, scalar=BIN[:, 8 + j:9 + j], in1=y, op0=ALU.add, op1=ALU.mult), t, t_b)
                    free(i3, t)
                    i4, p_z, t_z = product_T(b2, 1, 8, XH, XL, lo, W, None)
                    done_with(b2, t_z)
                    a4 = A.op(lambda e: e.activation(ZS[:, q, lo:W], p_z, ACT.Silu, bias=BIN[:, 24 + j:25 + j]),
                              t_z, yc_free[q] or xn)
                    free(i4, a4)
                    t = V.op(lambda e: e.tensor_tensor(y, y, ZS[:, q, lo:W], ALU.mult), t, a4)
                    t = split_to(CH[:, j, lo:W], CL[:, j, lo:W], y, t)
                    yc_free[q] = t
                    conv_done.append(t)

                pace[0] = P_GA
                ya = []
                for g in range(4):
                    b1 = block(8)
                    sg = []
                    for c in range(2):
                        j = 2 * g + c
                        i, p, t = product_T(b1, c, 8, XH, XL, lo, W, None)
                        sg.append(A.op(lambda e: e.activation(YA[:, j, lo:W], p, ACT.Sigmoid,
                                                              bias=BIN[:, 80 + j:81 + j]), t))
                        free(i, sg[-1])
                    done_with(b1, t)
                    b2 = block(8)
                    for c in range(2):
                        j = 2 * g + c
                        i, p, t = product_T(b2, c, 8, CH, CL, lo, W, conv_done)
                        v = V.op(lambda e: e.tensor_tensor(YA[:, j, lo:W], p, YA[:, j, lo:W], ALU.mult), t, sg[c])
                        free(i, v)
                        ya.append(v)
                    done_with(b2, t)
                conv_end = [t, ya[-1]]
                if grp == 1 and l == 0:
                    while 1 not in routed:
                        pump()
                    conv_end += now()

                pace[0] = P_HEAD
                m_cs = again("cs", SP, CS[:, :, 0:W], d["cos_sin"][:, :, 0:W] if grp == 0 else d["cos_sin"][:, :, WA:T],
                             conv_end)
                turn = {n: list(conv_end) for n in ("qk", "kp", "sx", "oo", "rh", "dt", "bv", "st")}
                turn["vv"] = conv_end + (parked or [])
                turn["z"] = list(conv_end)
                yb = [None] * 8

                def turn_rows(h, norm_done, z_done):
                    marks = []
                    for jj in (0, 2):
                        i = bank()
                        PE.wait(norm_done)
                        for j in (jj, jj + 1):
                            for b in range(2):
                                c = 256 * (j % 2) + 128 * b
                                fn = lambda e: e.transpose(PS[:, i, c:c + 128], OO[:, b, 128 * j:128 * j + 128],
                                                           I128[:, :])
                                t = PE.op(fn) if b and j % 2 else PE.quiet(fn)
                        for j in (jj, jj + 1):
                            c = 256 * (j % 2)
                            v = V.op(lambda e: e.scalar_tensor_tensor(
                                out=Z[:, j, xo:W], in0=PS[:, i, c:c + 256], scalar=GNG[:, 4 * h + j:4 * h + j + 1],
                                in1=Z[:, j, xo:W], op0=ALU.mult, op1=ALU.mult), t, z_done, m_gn)
                            marks.append(v)
                        free(i, v)
                        pump(0.3)
                    if meta_rows:
                        i = bank()
                        for j in range(4):
                            fn = lambda e: e.transpose(PS[:, i, NM * j:NM * j + NM], OO[0:NM, 2, 128 * j:128 * j + 128],
                                                       I128[0:NM, 0:NM])
                            t = PE.op(fn) if j == 3 else PE.quiet(fn)
                        for j in range(4):
                            v = V.op(lambda e: e.scalar_tensor_tensor(
                                out=Z[:, j, 0:NM], in0=PS[:, i, NM * j:NM * j + NM],
                                scalar=GNG[:, 4 * h + j:4 * h + j + 1], in1=Z[:, j, 0:NM],
                                op0=ALU.mult, op1=ALU.mult), t)
                            marks.append(v)
                        free(i, v)
                    turn["oo"] = [t]
                    out = split_to(RH[:, :, lo:W], RL[:, :, lo:W], Z[:, :, lo:W], marks, turn["rh"])
                    turn["z"] = [out]
                    return out

                def out_rows(h, ret_done):
                    for half in range(2):
                        blk = block(4)
                        for c in range(4):
                            j = 4 * half + c
                            i, p, t = product_T(blk, c, 4, RH, RL, lo, W, ret_done)
                            if h == 0:
                                v = A.op(lambda e: e.activation(YB[:, j, lo:W], p, ACT.Copy), t)
                            else:
                                v = V.op(lambda e: e.tensor_tensor(YB[:, j, lo:W], p, YB[:, j, lo:W], ALU.add), t, yb[j])
                            free(i, v)
                            yb[j] = v
                        done_with(blk, t)
                    turn["rh"] = [t]

                before = None
                for h in range(5):
                    if h < 4:
                        m_dt = again("dt", SP, DT[:, :], d["decay"][h], turn["dt"])
                        m_dm = again("dm", SP, DMT[:, 0:W],
                                     d["decay_meta"][h, :, 0:W] if grp == 0 else d["decay_meta"][h, :, WA:T], turn["dt"])
                        m_bv = again("bv", SP, BV[:, :],
                                     d["b_in"][l, 6144 + 512 * h:6656 + 512 * h].partition_broadcast(128), turn["bv"])
                        if grp == 1:
                            m_kp = again("kp", SP, KP[:, :, :], d["keys_seen"][l, h], turn["kp"], kept[("k", l, h)])
                            m_vp = again("vp", SP, VP[:, 0:2, :], d["values_seen"][l, h], turn["vv"], kept[("v", l, h)])
                            m_vq = again("vq", SP, VP[0:NM, 2, :], d["values_meta"][l, h], turn["vv"], kept[("w", l, h)])
                        qk = []
                        for n in range(2):
                            blk = block(8)
                            for c in range(2):
                                i, p, t = product_T(blk, c, 8, XH, XL, 0, W, None)
                                col = 32 + 8 * n + 2 * h + c
                                a = A.op(lambda e: e.activation(QK[:, 2 * n + c, 0:W], p, ACT.Identity,
                                                                bias=BIN[:, col:col + 1]), t, turn["qk"])
                                free(i, a)
                                qk.append(a)
                            done_with(blk, t)
                    if before is not None:
                        ret_done = turn_rows(h - 1, *before)
                    if h < 4:
                        one, two = QK[:, 0:4:2, 0:W], QK[:, 1:4:2, 0:W]
                        cos = CS[:, 0, 0:W].unsqueeze(1).broadcast_to([128, 2, W])
                        sin = CS[:, 1, 0:W].unsqueeze(1).broadcast_to([128, 2, W])
                        r_a, r_b, r_c = RP[:, 0, :, 0:W], RP[:, 1, :, 0:W], RP[:, 2, :, 0:W]
                        V.op(lambda e: e.tensor_tensor(r_a, one, cos, ALU.mult), qk, m_cs, turn["oo"])
                        t2 = V.op(lambda e: e.tensor_tensor(r_b, two, sin, ALU.mult), loose=True)
                        t3 = V.op(lambda e: e.tensor_tensor(r_c, one, sin, ALU.mult), loose=True)
                        t = V.op(lambda e: e.tensor_tensor(one, r_a, r_b, ALU.subtract), t2, t3)
                        t = V.op(lambda e: e.tensor_tensor(r_a, two, cos, ALU.mult), t)
                        rot = V.op(lambda e: e.tensor_tensor(two, r_c, r_a, ALU.add), t)
                        turn["qk"] = []
                        if grp == 0:
                            kept[("k", l, h)] = again(f"ks{h}", SP, d["keys_seen"][l, h], QK[:, 2:4, 0:W], rot)
                            turn["qk"].append(kept[("k", l, h)])
                        vm = []
                        for n in range(2):
                            blk = block(8)
                            i, p, t = product_rows(blk, XH, XL, [xo, xo + 128], None)
                            v = V.op(lambda e: e.tensor_tensor(
                                VV[:, 0:2, 256 * n:256 * n + 256], p,
                                BV[:, 256 * n:256 * n + 256].unsqueeze(1).broadcast_to([128, 2, 256]), ALU.add),
                                t, m_bv, turn["vv"])
                            free(i, v)
                            vm.append(v)
                            if grp == 0:
                                i, p, t = product_rows(blk, XH, XL, [0], None)
                                v = V.op(lambda e: e.tensor_tensor(
                                    VV[0:NM, 2, 256 * n:256 * n + 256], p[0:NM, 0, :],
                                    BV[0:NM, 256 * n:256 * n + 256], ALU.add), t)
                                free(i, v)
                                vm.append(v)
                            done_with(blk, t)
                        turn["bv"] = [v]
                        turn["vv"] = []
                        if grp == 0:
                            kept[("v", l, h)] = again(f"vs{h}", SP, d["values_seen"][l, h], VV[:, 0:2, :], vm)
                            kept[("w", l, h)] = again(f"ws{h}", SP, d["values_meta"][l, h], VV[0:NM, 2, :], vm)
                            turn["vv"] += [kept[("v", l, h)], kept[("w", l, h)]]
                    if before is not None:
                        out_rows(h - 1, ret_done)
                    if h == 4:
                        break
                    sm = []
                    own = [(512, QK[:, 2:4, xo:xo + 128], 0, 0), (768, QK[:, 2:4, xo + 128:xo + 256], 128, 0)]
                    sets = [own]
                    if grp == 1:
                        PE.wait(m_kp)
                        sets.insert(0, [(0, KP[:, :, NM:NM + 128], 0, 256), (256, KP[:, :, NM + 128:NM + 256], 0, 128)])
                    for keys in sets:
                        i = bank()
                        PE.wait(rot)
                        at_ = 0
                        for _, ks, q0, _ in keys:
                            for dk in range(2):
                                t = PE.op(matmul(PS[:, i, at_:at_ + 256 - q0], ks[:, dk, :], QK[:, dk, xo + q0:W],
                                                 dk == 0, dk == 1))
                            at_ += 256 - q0
                        at_ = 0
                        for sx, _, q0, dc in keys:
                            n = 256 - q0
                            v = V.op(lambda e: e.tensor_tensor(SX[:, sx:sx + n], PS[:, i, at_:at_ + n],
                                                               DT[:, dc:dc + n], ALU.mult), t, m_dt, turn["sx"])
                            at_ += n
                            sm.append(v)
                        free(i, v)
                        pump(0.5)
                    i = bank()
                    km = QK[:, 2:4, 0:NM] if grp == 0 else KP[:, :, 0:NM]
                    for dk in range(2):
                        t = PE.op(matmul(PS[0:NM, i, 0:W - lo], km[:, dk, :], QK[:, dk, lo:W], dk == 0, dk == 1))
                    turn["qk"].append(t)
                    turn["kp"] = [t]
                    v = V.op(lambda e: e.tensor_tensor(SM[:, lo:W], PS[0:NM, i, 0:W - lo], DMT[:, lo:W], ALU.mult),
                             t, m_dm, turn["sx"])
                    sm.append(v)
                    free(i, v)
                    turn["dt"] = [v]
                    zm = []
                    for n in range(2):
                        blk = block(8)
                        for c in range(2):
                            j = 2 * n + c
                            i, p, t = product_T(blk, c, 8, XH, XL, lo, W, None)
                            col = 64 + 4 * h + j
                            a = A.op(lambda e: e.activation(Z[:, j, lo:W], p, ACT.Silu, bias=BIN[:, col:col + 1]),
                                     t, m_bin, turn["z"])
                            free(i, a)
                            zm.append(a)
                        done_with(blk, t)
                    om = []
                    for b in (0, 1) + ((2,) if meta_rows else ()):
                        i = bank()
                        PE.wait(sm, vm)
                        rows = NM if b == 2 else 128
                        if b == 2:
                            t = PE.op(matmul(PS[0:NM, i, :], SM[:, 0:NM], VV[0:NM, 2, :], True, True))
                        else:
                            terms = [(SX[:, 512 + 128 * b:640 + 128 * b], VV[:, 0, :])]
                            if b == 1:
                                terms.append((SX[:, 768:896], VV[:, 1, :]))
                            if grp == 1:
                                PE.wait(m_vp, m_vq)
                                terms += [(SX[:, 256 * m + 128 * b:256 * m + 128 * b + 128], VP[:, m, :])
                                          for m in range(2)]
                            terms.append((SM[:, xo + 128 * b:xo + 128 * b + 128],
                                          (VV if grp == 0 else VP)[0:NM, 2, :]))
                            for n, (s_, m_) in enumerate(terms):
                                t = PE.op(matmul(PS[:, i, :], s_, m_, n == 0, n == len(terms) - 1))
                        a = A.op(lambda e: e.activation(OO[0:rows, b, :], PS[0:rows, i, :], ACT.Copy), t, rot,
                                 turn["oo"])
                        free(i, a)
                        om.append((rows, b, a))
                        pump(0.8)
                    turn["vv"].append(t)
                    turn["sx"] = [t]
                    norm = []
                    for rows, b, a in om:
                        v = V.op(lambda e: e.bn_stats(ST[0:rows, b, :], OO[0:rows, b, :]), a, turn["st"])
                        v = V.op(lambda e: e.bn_aggr(MV[0:rows, b, :], ST[0:rows, b, :]), v)
                        norm.append(V.op(lambda e: e.tensor_copy(SS[0:rows, b:b + 1], MV[0:rows, b, 1:2]), v))
                    r = root(1.0, GN_EPS, 3, norm)
                    nd = []
                    for rows, b, a in om:
                        v = V.op(lambda e: e.scalar_tensor_tensor(
                            out=MV[0:rows, b, 0:1], in0=MV[0:rows, b, 0:1], scalar=-1.0, in1=RS[0:rows, b:b + 1],
                            op0=ALU.mult, op1=ALU.mult), r)
                        nd.append(A.op(lambda e: e.activation(OO[0:rows, b, :], OO[0:rows, b, :], ACT.Identity,
                                                              bias=MV[0:rows, b, 0:1], scale=RS[0:rows, b:b + 1]), v))
                    turn["st"] = [nd[-1]]
                    before = (nd, zm)

                gone = turn["vv"]
                back = {}
                for b in range(2):
                    row = 256 * grp + 128 * b
                    src = d["x"] if l == 0 else d["rows"]
                    back[b] = again(f"hb{b}", SP, HW[:, b, :], src[row:row + 128, :], gone)
                if meta_rows:
                    back[2] = again("hb2", SP, HM[:, :], d["meta"], gone)
                m_g = again("gbc", SP, GBC[:, :], d["post_norm_g"][l].partition_broadcast(128), xn, gbc_free)

                pace[0] = P_GB
                ym = []
                tg_free = [None, None]
                heads_end = turn["rh"] + [yb[-1]]
                m_in = again("gb2", SP, GB2[:, :],
                             (d["pre_norm_g"][l + 1] if l + 1 < DEPTH else d["norm1_g_2"][0]).partition_broadcast(128),
                             heads_end)
                for g in range(4):
                    blk = block(8)
                    for c in range(2):
                        j = 2 * g + c
                        i, p, t = product_T(blk, c, 8, XH, XL, lo, W, None)
                        a = A.op(lambda e: e.activation(TG[:, c, lo:W], p, ACT.Sigmoid, bias=BIN[:, 88 + j:89 + j]),
                                 t, tg_free[c], heads_end)
                        free(i, a)
                        y = TG[:, c, lo:W]
                        v = V.op(lambda e: e.tensor_tensor(y, y, YB[:, j, lo:W], ALU.mult), a, yb[j])
                        v = V.op(lambda e: e.tensor_tensor(y, y, YA[:, j, lo:W], ALU.add), v, ya[j])
                        v = split_to(YH[:, j, lo:W], YL[:, j, lo:W], y, v, heads_end)
                        tg_free[c] = v
                        ym.append(v)
                    done_with(blk, t)
                x_used = t
                par_free = a
                A.op(lambda e: e.activation(RS[:, 7:8], SS[:, 7:8], ACT.Sqrt), m_ss, m_rs)
                pace[0] = P_WO
                sums, y2 = [], []
                for n in range(4):
                    blk = block(8)
                    i, p, t = product_rows(blk, YH, YL, [xo, xo + 128], ym)
                    c_ = slice(256 * n, 256 * n + 256)
                    if n == 2:
                        pace[0] = 0.0
                    for b in range(2):
                        a = A.op(lambda e: e.activation(JY[:, 0:256], p[:, b, :], ACT.Square,
                                                        accum_out=SSP[:, b, n:n + 1]), t)
                    v = V.op(lambda e: e.tensor_tensor(
                        Y2[:, :, c_], p, GBC[:, c_].unsqueeze(1).broadcast_to([128, 2, 256]), ALU.mult), a, m_g)
                    free(i, v)
                    sums.append(a)
                    y2.append(v)
                    if meta_rows:
                        i, p, t = product_rows(blk, YH, YL, [0], None)
                        a = A.op(lambda e: e.activation(JY[0:NM, 0:256], p[0:NM, 0, :], ACT.Square,
                                                        accum_out=SSP[0:NM, 2, n:n + 1]), t)
                        v = V.op(lambda e: e.tensor_tensor(Y2M[:, c_], p[0:NM, 0, :], GBC[0:NM, c_], ALU.mult), a)
                        free(i, v)
                        sums.append(a)
                        y2.append(v)
                    done_with(blk, t)
                gbc_free = y2
                v = V.op(lambda e: e.tensor_reduce(SS[:, 0:3], SSP[:, :, :], AX.X, ALU.add), sums, m_ss, m_ssp)
                r = root(1.0 / 1024, EPS, 3, v)
                r = V.op(lambda e: e.tensor_copy(RP3[:, :], RS[:, 0:3]), r)
                parked = []

                def residual(b, r=r, parked=parked, back=back, y2=y2):
                    rows = NM if b == 2 else 128
                    y, h_ = (Y2M[:, :], HM[:, :]) if b == 2 else (Y2[:, b, :], HW[:, b, :])
                    v = V.op(lambda e: e.scalar_tensor_tensor(
                        out=h_, in0=y, scalar=RP3[0:rows, b:b + 1], in1=h_, op0=ALU.mult, op1=ALU.add),
                        r, y2, back[b], loose=True)
                    if b < 2:
                        row = 256 * grp + 128 * b
                        parked.append(again(f"hs{b}", SP, d["rows"][row:row + 128, :], h_, v))
                    return v

                ready = {b: (lambda b=b, f=residual: f(b)) for b in range(3 if meta_rows else 2)}
                region_free = [x_used, t, y2[-1]]
            return x_tiles, ready, parked, region_free, m_in, xo, W

        def second(grp, x_tiles, ready, parked, region_free, m_in, xo, W):
            xn = transposed(x_tiles, GB2, m_in, ready, XT, JK, x_free=region_free)
            m_mk = again("mk", SP, MK[:, :, :], d["masks"], xn)
            m_wgl = again("wgl", SP, WGL[:, :, :], d["w_glow"], xn, parked)
            m_upw = again("upw", SP, UPW[:, :], d["gla_w_gate_up_2"][0], xn, parked)
            m_g2 = again("gbc", SP, GBC[:, :], d["norm2_g_2"][0].partition_broadcast(128), xn)
            if grp == 1:
                m_v2p = again("v2p", SP, V2P[:, :, :], d["values2_seen"], xn, kept["v2"])

            def tile256(blk, c, evac):
                i, p, t = product_T(blk, c, 8, XH, XL, xo, W, xn)
                m = evac(p, t)
                free(i, m)
                return m, t

            pace[0] = P_SECOND
            sd0 = V.op(lambda e: e.memset(SD[:, :, :], 0.0), xn)
            qm, km, fm = [None] * 6, [None] * 6, [None] * 6
            def low_rank():
                i = bank()
                PE.wait(xn, m_wgl, m_upw)
                for k in range(8):
                    for n, part in enumerate((XH, XL)):
                        t = PE.op(matmul(PS[0:16, i, 0:256], WGL[:, k, :], f32(part[:, k, xo:W]), k == 0 and n == 0,
                                         k == 7 and n == 1))
                a = A.op(lambda e: e.activation(GLT[:, :], PS[0:16, i, 0:256], ACT.Copy), t, parked)
                free(i, a)
                return a

            def gate(a):
                i = bank()
                PE.wait(a)
                for c in range(2):
                    t = PE.op(matmul(PS[:, i, 256 * c:256 * c + 256], UPW[:, 128 * c:128 * c + 128], GLT[:, :], True, True))
                gz, tmp, gt2 = F6[:, 4:6, :], G6[:, 4:6, :], G6[:, 2:4, :]
                for c in range(2):
                    a = A.op(lambda e: e.activation(F6[:, 4 + c, :], PS[:, i, 256 * c:256 * c + 256], ACT.Identity,
                                                    bias=VG[:, 2 + c:3 + c]), t, m_vg, xn)
                free(i, a)
                t = A.op(lambda e: e.activation(tmp, gz, ACT.Abs), a)
                t = A.op(lambda e: e.activation(tmp, tmp, ACT.Exp, scale=-1.0), t)
                t = V.op(lambda e: e.tensor_scalar(tmp, tmp, 1.0, None, ALU.add), t)
                t = A.op(lambda e: e.activation(gt2, tmp, ACT.Ln), t)
                t = V.op(lambda e: e.scalar_tensor_tensor(out=tmp, in0=gz, scalar=0.0, in1=gt2, op0=ALU.min,
                                                          op1=ALU.subtract), t)
                m_fg = A.op(lambda e: e.activation(gz, tmp, ACT.Exp, scale=1.0 / 16), t)

                return m_fg

            for g in range(2):
                blk = block(8)
                for c in range(2):
                    n = 2 * g + c
                    qm[n], t = tile256(blk, c, lambda p, t: A.op(
                        lambda e: e.activation(Q6[:, n, :], p, ACT.Silu), t))
                done_with(blk, t)
                if g == 0:
                    low = low_rank()
                else:
                    m_fg = gate(low)
                    fm[4] = fm[5] = m_fg
            for g in range(2):
                blk = block(8)
                for c in range(2):
                    n = 2 * g + c
                    s, t = tile256(blk, c, lambda p, t: A.op(
                        lambda e: e.activation(F6[:, n, :], p, ACT.Sigmoid), t))
                    fm[n] = V.op(lambda e: e.tensor_scalar(F6[:, n, :], F6[:, n, :], LB1[:, n:n + 1], LB[:, n:n + 1],
                                                           ALU.mult, ALU.add), s, m_lb)
                    km[n] = V.op(lambda e: e.tensor_scalar(K6[:, n, :], F6[:, n, :], -1.0, 1.0, ALU.mult, ALU.add),
                                 fm[n])
                done_with(blk, t)
            for dest, marks, scale in ((Q6, qm, 0.125), (K6, km, 1.0)):
                blk = block(8)
                for c in range(2):
                    marks[4 + c], t = tile256(blk, c, lambda p, t: A.op(
                        lambda e: e.activation(dest[:, 4 + c, :], p, ACT.Copy, scale=scale), t))
                done_with(blk, t)

            vmarks, gmarks, last_side = [], [None] * 8, [None]

            def rest():
                for g in range(4):
                    blk = block(8)
                    i, p, t = product_rows(blk, XH, XL, [xo, xo + 128], None)
                    a = A.op(lambda e: e.activation(V2[:, :, 256 * g:256 * g + 256], p, ACT.Copy), t, parked)
                    free(i, a)
                    vmarks.append(a)
                    done_with(blk, t)
                    last_side[0] = t
                    yield
                if grp == 0:
                    kept["v2"] = once(SP, d["values2_seen"], V2[:, :, :], vmarks)
                for g in range(4):
                    blk = block(8)
                    for c in range(2):
                        j = 2 * g + c
                        gmarks[j], t = tile256(blk, c, lambda p, t: A.op(
                            lambda e: e.activation(GT[:, j, :], p, ACT.Silu), t))
                        last_side[0] = t
                        if c == 1:
                            done_with(blk, t)
                        yield

            side = rest()

            units = [((0, 1), ((0, 1),)), ((2, 3), ((2, 3),)), ((4, 5), ((4,), (5,), (6,), (7,)))]
            sdm = [sd0] * 8
            som = []

            def operands(hh):
                g = hh if hh < 4 else 4 + (hh - 4) // 2
                rows = slice(0, 128) if hh < 4 else slice(64 * (hh % 2), 64 * (hh % 2) + 64)
                return g, rows

            def score(unit, pieces, width, evac, keys=None):
                for heads in unit[1]:
                    i = bank()
                    PE.wait([qm[g] for g in unit[0]], [km[g] for g in unit[0]])
                    for q, hh in enumerate(heads):
                        g, rows = operands(hh)
                        for col, (k0, k1), (q0, q1) in pieces:
                            t = PE.op(matmul(PS[:, i, width * q + col:width * q + col + q1 - q0],
                                             (K6 if keys is None else keys)[rows, g, k0:k1], Q6[rows, g, q0:q1],
                                             True, True))
                    free(i, evac(heads, i, t))
                return t

            def masked(level):
                def evac(heads, i, t):
                    n = 2 * len(heads)
                    m = V.op(lambda e: e.copy_predicated(
                        SD[:, heads[0]:heads[0] + len(heads), :].rearrange("p h (b q) -> p (h b) q", b=2),
                        MK[:, level, :].bitcast(U32).unsqueeze(1).broadcast_to([128, n, 128]),
                        PS[:, i, 0:128 * n].rearrange("p (b q) -> p b q", b=n)), t, m_mk, [sdm[x] for x in heads], loose=True)
                    for x in heads:
                        sdm[x] = m
                    return m
                return evac

            def plain(dest, n):
                def evac(heads, i, t):
                    m = A.op(lambda e: e.activation(dest(heads), PS[:, i, 0:n * len(heads)], ACT.Copy), t,
                             last_side[0], xn)
                    som.append(m)
                    return m
                return evac

            diag = [(128 * b, (128 * b, 128 * b + 128), (128 * b, 128 * b + 128)) for b in range(2)]

            def merged(x, unit):
                a = unit[0][0]
                return x[:, a:a + 2, :].rearrange("p g t -> p (g t)")

            for unit in units:
                done = score(unit, diag, 256, masked(0))
                q_ = merged(Q6, unit)
                m = V.op(lambda e: e.tensor_tensor(q_, q_, merged(F6, unit), ALU.mult),
                             done, [fm[g] for g in unit[0]], [qm[g] for g in unit[0]], loose=True)
                for g in unit[0]:
                    qm[g] = m
                next(side, None)
                pump()
            goff = 0
            tm = {unit[0]: [fm[g] for g in unit[0]] for unit in units}
            for lv in range(8):
                s = 1 << lv
                for unit in units:
                    if s <= 64:
                        done = score(unit, diag, 256, masked(lv + 1))
                    else:
                        done = score(unit, [(0, (0, 128), (128, 256))], 128, plain(
                            lambda heads: S1[:, heads[0]:heads[0] + len(heads), :].rearrange("p h q -> p (h q)"), 128))
                    n = 256 // s
                    tv = F6 if s == 1 else G6
                    a = unit[0][0]
                    tv = tv[:, a:a + 2, :] if s == 1 else tv[:, a:a + 2, goff:goff + n]
                    tv = tv.rearrange("p g (c two) -> p g c two", two=2)
                    nxt = 0 if s == 1 else goff + n
                    q4 = Q6[:, a:a + 2, :].rearrange("p g (c two s) -> p g c two s", two=2, s=s)[:, :, :, 1, :]
                    k4 = K6[:, a:a + 2, :].rearrange("p g (c two s) -> p g c two s", two=2, s=s)[:, :, :, 0, :]
                    left = tv[:, :, :, 0:1].broadcast_to([128, 2, n // 2, s])
                    right = tv[:, :, :, 1:2].broadcast_to([128, 2, n // 2, s])
                    qmark = V.op(lambda e: e.tensor_tensor(q4, q4, left, ALU.mult), done, tm[unit[0]],
                                 [qm[g] for g in unit[0]], loose=True)
                    kmark = V.op(lambda e: e.tensor_tensor(k4, k4, right, ALU.mult), [km[g] for g in unit[0]],
                                 loose=True)
                    for g in unit[0]:
                        qm[g], km[g] = qmark, kmark
                    if s < 128:
                        tm[unit[0]] = [V.op(lambda e: e.tensor_tensor(
                            G6[:, a:a + 2, nxt:nxt + n // 2], tv[:, :, :, 0], tv[:, :, :, 1], ALU.mult),
                            m_fg, tm[unit[0]], loose=True)]
                    pump()
                    if unit is not units[1]:
                        next(side, None)
                goff = 0 if s == 1 else goff + 256 // s
                if grp == 1 and lv == 0:
                    m_k2 = once(SP, F6[:, :, :], d["keys2_seen"], kept["k2"], km, qm, list(tm.values()))
            for _ in side:
                pass
            if grp == 0:
                kept["k2"] = once(SP, d["keys2_seen"], K6[:, :, :], km)
                levels_used = [done, kept["k2"]]
            else:
                PE.wait(m_k2)
                for unit in units:
                    done = score((unit[0], tuple((x,) for hs in unit[1] for x in hs)),
                                 [(0, (0, 128), (0, 256)), (256, (128, 256), (0, 256))], 512, plain(
                        lambda heads: S2[:, heads[0], :, :].rearrange("p k q -> p (k q)"), 512), keys=F6)
                levels_used = [done]

            mixed = []
            PE.wait(sdm, som, vmarks)
            if grp == 1:
                PE.wait(m_v2p)
            units = [(b, half) for b in range(2) for half in range(2)]
            out_of, turned, joined = {}, {}, {}

            def weigh_values(u):
                b, half = units[u]
                i = bank()
                for q in range(4):
                    hh = 4 * half + q
                    c = slice(128 * hh, 128 * hh + 128)
                    terms = [(SD[:, hh, 128 * b:128 * b + 128], V2[:, b, c])]
                    if b == 1:
                        terms.append((S1[:, hh, :], V2[:, 0, c]))
                    if grp == 1:
                        terms += [(S2[:, hh, m, 128 * b:128 * b + 128], V2P[:, m, c]) for m in range(2)]
                    for n, (s_, m_) in enumerate(terms):
                        t = PE.op(matmul(PS[:, i, 128 * q:128 * q + 128], s_, m_, n == 0, n == len(terms) - 1))
                out_of[u] = t
                ss, rs = SS[:, 4 * (u % 2):4 * (u % 2) + 4], RS[:, 4 * (u % 2):4 * (u % 2) + 4]
                sq = SQ[:, 512 * (u % 2):512 * (u % 2) + 512]
                a = A.op(lambda e: e.activation(sq, PS[:, i, :], ACT.Square), t, levels_used)
                v = V.op(lambda e: e.tensor_reduce(ss, sq.rearrange("p (h v) -> p h v", h=4), AX.X, ALU.add), a)
                v = V.op(lambda e: e.tensor_scalar(ss, ss, 1.0 / 128, EPS, ALU.mult, ALU.add), v)
                a = A.op(lambda e: e.activation(rs, ss, ACT.Sqrt), v)
                v = V.op(lambda e: e.reciprocal(rs, rs), a)
                v = V.op(lambda e: e.tensor_tensor(
                    OT[:, 512 * (u % 2):512 * (u % 2) + 512].rearrange("p (h v) -> p h v", h=4),
                    PS[:, i, :].rearrange("p (h v) -> p h v", h=4),
                    rs.unsqueeze(2).broadcast_to([128, 4, 128]), ALU.mult), v, turned.get(u - 2))
                free(i, v)
                joined[u] = v
                pump(0.5)

            def turn_values(u):
                b, half = units[u]
                i = bank()
                PE.wait(joined[u])
                for j in range(4):
                    o = 512 * (u % 2) + 128 * j
                    t = PE.op(lambda e: e.transpose(PS[:, i, 128 * j:128 * j + 128], OT[:, o:o + 128], I128[:, :]))
                turned[u] = t
                gv = GT[:, 4 * half:4 * half + 4, 128 * b:128 * b + 128]
                v = V.op(lambda e: e.scalar_tensor_tensor(
                    out=gv, in0=PS[:, i, :].rearrange("p (j q) -> p j q", j=4),
                    scalar=VG[:, half:half + 1], in1=gv, op0=ALU.mult, op1=ALU.mult), t, gmarks, m_vg)
                free(i, v)
                sl = slice(4 * half, 4 * half + 4)
                mixed.append(split_to(MH[:, sl, 128 * b:128 * b + 128], ML[:, sl, 128 * b:128 * b + 128], gv, v,
                                      levels_used))

            weigh_values(0)
            weigh_values(1)
            turn_values(0)
            weigh_values(2)
            turn_values(1)
            weigh_values(3)
            turn_values(2)
            turn_values(3)
            v_used = out_of[3]
            back = [again(f"hb{b}", SP, HW[:, b, :], d["rows"][256 * grp + 128 * b:256 * grp + 128 * b + 128, :],
                          v_used, m_fg, kept["v2"]) for b in range(2)]
            hr = res[grp]
            hmk = list(back)
            for n in range(4):
                blk = block(8)
                i, p, t = product_rows(blk, MH, ML, [0, 128], mixed)
                cs_ = slice(256 * n, 256 * n + 256)
                v = V.op(lambda e: e.tensor_tensor(hr[:, :, cs_], HW[:, :, cs_], p, ALU.add), t, back)
                free(i, v)
                hmk.append(v)
                done_with(blk, t)
            out_used = t
            hm_all[grp] = hmk
            if grp == 0:
                fetched.append(rows_in(1, hmk))

            m_kt = again("kt", SP, KT[:, :, :], d["keys_T"], out_used, mixed)
            hn = hn_of[grp]
            tiles = [(128, hr[:, b, :], xo + 128 * b, b) for b in range(2)]
            xn2 = transposed(tiles, GBC, m_g2, {b: hmk for b in range(2)}, None,
                             SC[:, 0:8, :].rearrange("p a b -> p (a b)"), keep=hn,
                             x_free=[out_used, v_used] + mixed)
            hn_ready[grp] = xn2
            pace[0] = P_QP
            tops, late = [None, None], [[], []]
            prior = [(V.sem, V.n)]

            def look(g, marks):
                sc = sub_scores(g, marks, m_kt, xn2)
                for b in range(2):
                    if grp == 0 or b == 0:
                        tops[b] = top_keys(b, g, sc[b], prior)
                    else:
                        late[b].append((g, sc[b], prior))

            held = None
            for g in range(8):
                blk = block(8)
                qpm = []
                for c in range(2):
                    i, p, t = product_T(blk, c, 8, XH, XL, xo, W, xn2)
                    a = A.op(lambda e: e.activation(QP[:, 2 * g + c, :], p, ACT.Copy), t, xn2)
                    free(i, a)
                    qpm.append(a)
                done_with(blk, t)
                if held:
                    look(*held)
                held = (g, qpm)
            look(*held)
            return [route(2 * grp + b, tops[b], late[b]) for b in range(2)]

        kept = {}
        r_a, r_b = second(0, *layers(0))
        passed += now()
        stream = gathers([0, 1, 2, 3])
        taken = [0]

        def take(n=1):
            for _ in range(n):
                if taken[0] < 256:
                    next(stream)
                    taken[0] += 1

        def beside():
            yield from r_a
            for cost in r_b:
                yield cost
                if taken[0] < 100:
                    take()
                    yield PAIR_COST
            while taken[0] < EARLY:
                take()
                yield PAIR_COST

        background.append(beside())
        r_c, r_d = second(1, *layers(1))
        for _ in background[0] if background else ():
            pass
        shared[0] = False
        for _ in r_c:
            take()
        take(256)
        for cost in r_d:
            for _ in range(LATE):
                next(stream)
        for _ in stream:
            pass
        SP.wait(out_marks)


def _tables():
    import numpy as np
    half = 128
    inv = (10000.0 ** (-np.arange(half, dtype=np.float32) / half)).astype(np.float32)
    ang = (np.arange(T, dtype=np.float32)[:, None] * inv[None, :]).astype(np.float32)
    cs = np.stack([np.cos(ang).T, np.sin(ang).T], 1).astype(np.float32)
    lg = np.log(1.0 - 2.0 ** (-5.0 - np.arange(4, dtype=np.float64)))
    m = np.arange(128)[:, None]
    n = np.arange(512)[None, :]
    same = (m // 64 == n // 64) & (n < 128)
    seen = (m // 64 < n // 64) | (n >= 128)
    dist = np.where(same, np.abs(n - m), n - m)
    dec = np.exp(lg[:, None, None] * np.maximum(dist, 0)) * (same | seen) / 16.0
    mm = np.arange(NM)[:, None]
    nn = np.arange(T)[None, :]
    decm = np.exp(lg[:, None, None] * np.abs(nn - mm)) / 16.0
    masks = np.zeros((128, 8, 128), np.float32)
    j = np.arange(128)[:, None]
    i = np.arange(128)[None, :]
    masks[:, 0, :] = i == j
    for lv in range(7):
        s = 1 << lv
        masks[:, lv + 1, :] = (i // (2 * s) == j // (2 * s)) & (i // s % 2 == 1) & (j // s % 2 == 0)
    return {
        "ident": np.eye(128, dtype=np.float32),
        "cos_sin": np.ascontiguousarray(cs),
        "decay": dec.astype(np.float32),
        "decay_meta": decm.astype(np.float32),
        "masks": masks,
        "iota": np.arange(16, dtype=np.float32),
    }


def _layout(w):
    import numpy as np
    out = {}

    def kn(m):
        k = m.shape[0] // 128
        return k, m.reshape(k, 128, m.shape[1]).transpose(1, 0, 2)

    blocks = []
    for l in range(DEPTH):
        wi = w["w_in"][l]
        for j in range(8):
            a = 128 * j
            blocks.append(kn(np.concatenate([wi[:, a:a + 128], wi[:, 2048 + a:2176 + a]], 1)))
            blocks.append(kn(np.concatenate([wi[:, 1024 + a:1152 + a], wi[:, 3072 + a:3200 + a]], 1)))
        for g in range(4):
            blocks.append(kn(wi[:, 10240 + 256 * g:10496 + 256 * g]))
            blocks.append(kn(w["w_conv_out"][l][:, 256 * g:256 * g + 256]))
        def ret(h):
            m = w["w_ret_out"][l][512 * h:512 * h + 512]
            return [kn(m[:, 0:512]), kn(m[:, 512:1024])]
        for h in range(4):
            blocks.append(kn(wi[:, 4096 + 256 * h:4352 + 256 * h]))
            blocks.append(kn(wi[:, 5120 + 256 * h:5376 + 256 * h]))
            blocks.append(kn(wi[:, 6144 + 512 * h:6400 + 512 * h]))
            blocks.append(kn(wi[:, 6400 + 512 * h:6656 + 512 * h]))
            if h > 0:
                blocks += ret(h - 1)
            blocks.append(kn(wi[:, 8192 + 512 * h:8448 + 512 * h]))
            blocks.append(kn(wi[:, 8448 + 512 * h:8704 + 512 * h]))
        blocks += ret(3)
        for g in range(4):
            blocks.append(kn(wi[:, 11264 + 256 * g:11520 + 256 * g]))
        for g in range(4):
            blocks.append(kn(w["w_o"][l][:, 256 * g:256 * g + 256]))
    w2 = w["w_in_2"][0]
    starts = [0, 256, 512, 768, 2048, 2304, 1024, 1280, 2560, 2816, 1536, 1792, 3088, 3344]
    for a in starts:
        blocks.append(kn(w2[:, a:a + 256]))
    for g in range(4):
        blocks.append(kn(w["w_out_2"][0][:, 256 * g:256 * g + 256]))
    for g in range(8):
        blocks.append(kn(w["peer_w_q_2"][0][:, 256 * g:256 * g + 256]))
    halves = []
    for k, b in blocks:
        halves.append(b.reshape(128, k, 2, 1024 // k).transpose(2, 0, 1, 3).reshape(2, 128, 1024))
    out["halves"] = np.concatenate(halves)
    assert len(blocks) == DEPTH * BLOCKS_LAYER + BLOCKS_SECOND

    def tiles(v):
        return np.ascontiguousarray(v.reshape(-1, 128).T)

    out["x"] = np.ascontiguousarray(w["x"][0])
    out["meta"] = w["meta"]
    out["pre_norm_g"] = w["pre_norm_g"]
    out["post_norm_g"] = w["post_norm_g"]
    out["b_in"] = w["b_in"]
    out["b_in_T"] = np.stack([tiles(w["b_in"][l]) for l in range(DEPTH)])
    out["conv_w_T"] = np.stack([tiles(w["conv_w"][l]) for l in range(DEPTH)])
    out["conv_b_T"] = np.stack([tiles(w["conv_b"][l]) for l in range(DEPTH)])
    out["gn_g_T"] = np.stack([tiles(w["ret_gn_g"][l]) for l in range(DEPTH)])
    out["norm1_g_2"] = w["norm1_g_2"]
    out["norm2_g_2"] = w["norm2_g_2"]
    out["norm_f_g_2"] = w["norm_f_g_2"]
    out["logits_T"] = tiles(w["hg_lower_logits_2"])
    out["small_T"] = np.ascontiguousarray(np.concatenate(
        [tiles(w["hg_norm_g_2"]), tiles(w["gla_norm_g_2"]), tiles(w["gla_b_gate_2"])], 1))
    out["w_glow"] = np.ascontiguousarray(w2[:, 3072:3088].reshape(8, 128, 16).transpose(1, 0, 2))
    out["gla_w_gate_up_2"] = w["gla_w_gate_up_2"]
    out["keys_T"] = np.ascontiguousarray(w["peer_sub_keys_2"][0].reshape(16, 128, 128).transpose(2, 0, 1))
    out["peer_u_2"] = w["peer_u_2"][0]
    out["peer_v_2"] = w["peer_v_2"][0]
    return out


def kernel(**inputs):
    import numpy as np
    import concourse.bacc as bacc
    from concourse.bass_utils import run_bass_kernel_spmd

    arrays = dict(_layout({k: np.asarray(v) for k, v in inputs.items()}))
    arrays.update(_tables())
    nc = bacc.Bacc("TRN2", target_bir_lowering=False, num_devices=1)
    feeds, d = {}, {}
    for name, a in arrays.items():
        a = np.ascontiguousarray(a)
        feeds["in_" + name] = a
        d[name] = nc.dram_tensor("in_" + name, a.shape, mybir.dt.from_np(a.dtype), kind="ExternalInput").ap()
    for name, shape in (("rows", (512, 1024)), ("keys_seen", (DEPTH, 4, 128, 2, WA)),
                        ("values_seen", (DEPTH, 4, 128, 2, 512)), ("values_meta", (DEPTH, 4, NM, 512)),
                        ("keys2_seen", (128, 6, 256)), ("values2_seen", (128, 2, 1024))):
        d[name] = nc.dram_tensor(name, shape, F32, kind="Internal").ap()
    d["out"] = nc.dram_tensor("out_0", (512, 1024), F32, kind="ExternalOutput").ap()
    two_blocks(nc, d)
    r = run_bass_kernel_spmd(nc, [feeds], core_ids=[0])
    return np.asarray(r.results[0]["out_0"]).reshape(1, 512, 1024)
```
